# Optimizing a Trainium2 kernel written in Bass

```python
import jax, jax.numpy as jnp
from jax import lax
import numpy as np

D_MODEL = 1024
BATCH = 1
SEQ = 256
DEPTH = 1

CHUNK = 64
Q_BLOCK = 128
MEM_LEN = 256
D_MIX = D_MODEL
MLA_HEADS = 8
MLA_NOPE = 64
MLA_ROPE = 32
MLA_V = 64
MLA_WIDTH = MLA_HEADS * MLA_V
Q_LORA = 256
KV_LORA = 128
ROPE_THETA = 10000.0
CONV_CH = D_MIX - MLA_WIDTH
CONV_WIDTH = 31
IN_COLS = Q_LORA + KV_LORA + MLA_ROPE + 2 * CONV_CH
X_HEADS = 4
X_HEAD_DIM = D_MODEL // X_HEADS
N_EXPERTS = 32
TOP_K = 4
D_FF_EXPERT = D_MODEL
SWIGLU_LIMIT = 7.0
SWIGLU_ALPHA = 1.702
MOE_BLOCK = 256
NORM_EPS = 1e-5
MAX_OFFSET = 4096

kernel_name = "hybrid_mla_conformer_memxattn_moe"

def rmsnorm(x, g):
    xf = x.astype(jnp.float32)
    y = xf * lax.rsqrt(jnp.mean(xf * xf, axis=-1, keepdims=True) + NORM_EPS)
    return (y * g.astype(jnp.float32)).astype(x.dtype)

def layernorm(x, g, b):
    xf = x.astype(jnp.float32)
    mu = jnp.mean(xf, axis=-1, keepdims=True)
    var = jnp.mean(jnp.square(xf - mu), axis=-1, keepdims=True)
    y = (xf - mu) * lax.rsqrt(var + NORM_EPS)
    return (y * g.astype(jnp.float32) + b.astype(jnp.float32)).astype(x.dtype)

def rope_angles(pos):
    inv = ROPE_THETA ** (-jnp.arange(0, MLA_ROPE, 2, dtype=jnp.float32) / MLA_ROPE)
    ang = pos.astype(jnp.float32)[..., None] * inv
    return jnp.cos(ang), jnp.sin(ang)

def apply_rope(x, cos, sin):
    half = x.shape[-1] // 2
    x1 = x[..., :half].astype(jnp.float32)
    x2 = x[..., half:].astype(jnp.float32)
    return jnp.concatenate([x1 * cos - x2 * sin, x1 * sin + x2 * cos], axis=-1).astype(x.dtype)

def mla_attention(c_q, c_kv, k_rope_raw, pos, g_q, w_uq, g_kv, w_ukv):
    B, S, _ = c_q.shape
    q = (rmsnorm(c_q, g_q) @ w_uq).reshape(B, S, MLA_HEADS, MLA_NOPE + MLA_ROPE)
    q_nope, q_rope = q[..., :MLA_NOPE], q[..., MLA_NOPE:]
    kv = (rmsnorm(c_kv, g_kv) @ w_ukv).reshape(B, S, MLA_HEADS, MLA_NOPE + MLA_V)
    k_nope, v = kv[..., :MLA_NOPE], kv[..., MLA_NOPE:]
    cos, sin = rope_angles(pos)
    q_rope = apply_rope(q_rope, cos[:, :, None, :], sin[:, :, None, :])
    k_rope = apply_rope(k_rope_raw, cos, sin)
    scale = (MLA_NOPE + MLA_ROPE) ** -0.5
    chunk_id = jnp.arange(S) // CHUNK
    outs = []
    for blk in range(S // Q_BLOCK):
        q0, q1 = blk * Q_BLOCK, (blk + 1) * Q_BLOCK
        s = (jnp.einsum('bqhd,bkhd->bhqk', q_nope[:, q0:q1], k_nope[:, :q1])
             + jnp.einsum('bqhr,bkr->bhqk', q_rope[:, q0:q1], k_rope[:, :q1]))
        s = s.astype(jnp.float32) * scale
        mask = chunk_id[None, :q1] <= chunk_id[q0:q1, None]
        s = jnp.where(mask[None, None], s, -jnp.inf)
        p = jax.nn.softmax(s, axis=-1).astype(v.dtype)
        outs.append(jnp.einsum('bhqk,bkhd->bqhd', p, v[:, :q1]))
    return jnp.concatenate(outs, axis=1).reshape(B, S, MLA_WIDTH)

def conformer_conv(u, w_dw, b_dw, g_ln, b_ln):
    a, gate = u[..., :CONV_CH], u[..., CONV_CH:]
    z = a * jax.nn.sigmoid(gate)
    z = lax.conv_general_dilated(
        z, w_dw[:, None, :], window_strides=(1,), padding=[(CONV_WIDTH - 1, 0)],
        dimension_numbers=('NWC', 'WIO', 'NWC'), feature_group_count=CONV_CH) + b_dw
    return jax.nn.silu(layernorm(z, g_ln, b_ln))

def memory_cross_attention(h, mem_n, w_xq, w_xkv, w_xo):
    B, S, _ = h.shape
    M = mem_n.shape[1]
    q = (h @ w_xq).reshape(B, S, X_HEADS, X_HEAD_DIM)
    kv = (mem_n @ w_xkv).reshape(B, M, 2, X_HEADS, X_HEAD_DIM)
    k, v = kv[:, :, 0], kv[:, :, 1]
    s = jnp.einsum('bqhd,bmhd->bhqm', q, k).astype(jnp.float32) * (X_HEAD_DIM ** -0.5)
    p = jax.nn.softmax(s, axis=-1).astype(v.dtype)
    o = jnp.einsum('bhqm,bmhd->bqhd', p, v).reshape(B, S, D_MODEL)
    return o @ w_xo

def moe_ffn(h, w_router, b_router, w_up, b_up, w_down, b_down):
    B, S, D = h.shape
    N = B * S
    t = h.reshape(N, D)
    logits = (t @ w_router + b_router).astype(jnp.float32)
    top_val, top_idx = lax.top_k(logits, TOP_K)
    gates = jax.nn.softmax(top_val, axis=-1)
    A = N * TOP_K
    flat_e = top_idx.reshape(A)
    flat_tok = jnp.repeat(jnp.arange(N, dtype=jnp.int32), TOP_K)
    flat_g = gates.reshape(A)
    order = jnp.argsort(flat_e)
    se = flat_e[order]
    counts = jnp.bincount(flat_e, length=N_EXPERTS)
    start = jnp.cumsum(counts) - counts
    padded = (counts + MOE_BLOCK - 1) // MOE_BLOCK * MOE_BLOCK
    pend = jnp.cumsum(padded)
    pstart = pend - padded
    dest = pstart[se] + (jnp.arange(A) - start[se])
    P = A + N_EXPERTS * MOE_BLOCK
    nb = P // MOE_BLOCK
    slot_tok = jnp.full((P,), N, dtype=jnp.int32).at[dest].set(flat_tok[order])
    slot_gate = jnp.zeros((P,), jnp.float32).at[dest].set(flat_g[order])
    blk_e = jnp.minimum(jnp.searchsorted(pend, jnp.arange(nb) * MOE_BLOCK, side='right'),
                        N_EXPERTS - 1)
    t_pad = jnp.concatenate([t, jnp.zeros((1, D), t.dtype)], axis=0)

    def expert_block(args):
        tok, e = args
        xb = t_pad[tok]
        up = xb @ w_up[e] + b_up[e]
        glu, lin = up[:, :D_FF_EXPERT], up[:, D_FF_EXPERT:]
        glu = jnp.minimum(glu, SWIGLU_LIMIT)
        lin = jnp.clip(lin, -SWIGLU_LIMIT, SWIGLU_LIMIT)
        act = glu * jax.nn.sigmoid(SWIGLU_ALPHA * glu) * (lin + 1)
        return act @ w_down[e] + b_down[e]

    y = lax.map(expert_block, (slot_tok.reshape(nb, MOE_BLOCK), blk_e))
    y = y.reshape(P, D) * slot_gate[:, None].astype(y.dtype)
    out = jax.ops.segment_sum(y, slot_tok, num_segments=N + 1)[:N]
    return out.reshape(B, S, D)

def setup_inputs(seed: int = 0) -> dict:
    key = jax.random.key(seed)
    ks = jax.random.split(key, 32)
    f32 = jnp.float32
    L = DEPTH

    def w(k, shape, fan_in):
        return jax.random.normal(k, shape, f32) * (fan_in ** -0.5)

    def gain(k, shape):
        return 1.0 + 0.02 * jax.random.normal(k, shape, f32)

    def bias(k, shape):
        return 0.01 * jax.random.normal(k, shape, f32)

    x = jax.random.normal(ks[0], (BATCH, SEQ, D_MODEL), f32)
    mem = jax.random.normal(ks[1], (BATCH, MEM_LEN, D_MODEL), f32)
    offs = jax.random.randint(ks[2], (BATCH, 1), 0, MAX_OFFSET, dtype=jnp.int32)
    positions = offs + jnp.arange(SEQ, dtype=jnp.int32)[None, :]
    return {
        "x": x,
        "mem": mem,
        "positions": positions,
        "g_mix": gain(ks[3], (L, D_MODEL)),
        "w_in": w(ks[4], (L, D_MODEL, IN_COLS), D_MODEL),
        "g_q": gain(ks[5], (L, Q_LORA)),
        "w_uq": w(ks[6], (L, Q_LORA, MLA_HEADS * (MLA_NOPE + MLA_ROPE)), Q_LORA),
        "g_kv": gain(ks[7], (L, KV_LORA)),
        "w_ukv": w(ks[8], (L, KV_LORA, MLA_HEADS * (MLA_NOPE + MLA_V)), KV_LORA),
        "w_dw": w(ks[9], (L, CONV_WIDTH, CONV_CH), CONV_WIDTH),
        "b_dw": bias(ks[10], (L, CONV_CH)),
        "g_conv_ln": gain(ks[11], (L, CONV_CH)),
        "b_conv_ln": bias(ks[12], (L, CONV_CH)),
        "w_out": w(ks[13], (L, D_MIX, D_MODEL), D_MIX),
        "g_xattn": gain(ks[14], (L, D_MODEL)),
        "g_mem": gain(ks[15], (L, D_MODEL)),
        "w_xq": w(ks[16], (L, D_MODEL, D_MODEL), D_MODEL),
        "w_xkv": w(ks[17], (L, D_MODEL, 2 * D_MODEL), D_MODEL),
        "w_xo": w(ks[18], (L, D_MODEL, D_MODEL), D_MODEL),
        "g_ffn": gain(ks[19], (L, D_MODEL)),
        "w_router": w(ks[20], (L, D_MODEL, N_EXPERTS), D_MODEL),
        "b_router": bias(ks[21], (L, N_EXPERTS)),
        "w_up": w(ks[22], (L, N_EXPERTS, D_MODEL, 2 * D_FF_EXPERT), D_MODEL),
        "b_up": bias(ks[23], (L, N_EXPERTS, 2 * D_FF_EXPERT)),
        "w_down": w(ks[24], (L, N_EXPERTS, D_FF_EXPERT, D_MODEL), D_FF_EXPERT),
        "b_down": bias(ks[25], (L, N_EXPERTS, D_MODEL)),
        "g_final": gain(ks[26], (D_MODEL,)),
    }

def reference(x, mem, positions, g_mix, w_in, g_q, w_uq, g_kv, w_ukv, w_dw, b_dw,
              g_conv_ln, b_conv_ln, w_out, g_xattn, g_mem, w_xq, w_xkv, w_xo,
              g_ffn, w_router, b_router, w_up, b_up, w_down, b_down, g_final):
    o1 = Q_LORA
    o2 = o1 + KV_LORA
    o3 = o2 + MLA_ROPE
    for l in range(DEPTH):
        h = rmsnorm(x, g_mix[l])
        u = h @ w_in[l]
        y_mla = mla_attention(u[..., :o1], u[..., o1:o2], u[..., o2:o3], positions,
                              g_q[l], w_uq[l], g_kv[l], w_ukv[l])
        y_conv = conformer_conv(u[..., o3:], w_dw[l], b_dw[l], g_conv_ln[l], b_conv_ln[l])
        x = x + jnp.concatenate([y_mla, y_conv], axis=-1) @ w_out[l]
        x = x + memory_cross_attention(rmsnorm(x, g_xattn[l]), rmsnorm(mem, g_mem[l]),
                                       w_xq[l], w_xkv[l], w_xo[l])
        x = x + moe_ffn(rmsnorm(x, g_ffn[l]), w_router[l], b_router[l],
                        w_up[l], b_up[l], w_down[l], b_down[l])
    return rmsnorm(x, g_final)


_drawn_inputs = setup_inputs


def setup_inputs(seed=0):
    import zlib

    import numpy as np

    out = dict(_drawn_inputs(seed))
    spreads = {}
    factors = {'g_q': 4.188,
     'g_kv': 5.365,
     'b_conv_ln': 20.251,
     'g_xattn': 24.73,
     'b_up': 34.028,
     'b_down': 39.333,
     'g_final': 7.86,
     'b_dw': 8.0,
     'g_conv_ln': 7.451,
     'g_mem': 3.831,
     'g_ffn': 3.937,
     'b_router': 7.729}
    for name, (base, spread) in spreads.items():
        noise = np.random.default_rng([zlib.crc32(name.encode()), seed]).standard_normal(out[name].shape)
        drawn = base * np.exp(spread * noise) if base else spread * noise
        out[name] = __import__('jax').numpy.asarray(drawn.astype(out[name].dtype))
    for name, factor in factors.items():
        out[name] = (out[name] * factor).astype(out[name].dtype)
    return out
```

```python
import numpy as np
import concourse.bass as bass
from concourse import mybir
from contextlib import ExitStack

D = 1024
T = 256
M = 256
P = 128
KT = D // P
TT = T // P
CHUNK = 64
HEADS, NOPE, ROPE, VDIM = 8, 64, 32, 64
QK = NOPE + ROPE
Q_LORA, KV_LORA = 256, 128
CONV, TAPS = 512, 31
CT = CONV // P
TOK_COLS = Q_LORA + KV_LORA + ROPE
IN_COLS = TOK_COLS + 2 * CONV
XH, XD = 4, 256
E, TOPK, FF = 32, 4, 1024
CAP = 64
LIMIT, ALPHA = 7.0, 1.702
EPS = 1e-5
ROPE_THETA = 10000.0
MASKED = -1e30
ABSENT = 4096.0
SLAB = 2 * D
BANK = 512


def trunk_jobs():
    jobs = [("vec", "v", "v")]
    jobs += [(f"hT{i}", "v", "v") for i in range(4)]
    jobs += [(f"u{t}", "v", "v") for t in range(2)]
    jobs += [(f"mT{i}", "a", "a") for i in range(4)]
    jobs += [(f"cv{c}", "a", "v") for c in range(4)]
    jobs += [("cqT", "v", "v"), ("ckvT", "v", "v"), ("krT", "a", "a")]
    jobs += [(f"q{t}{h}", "a", "a") for t in range(2) for h in range(2)]
    jobs += [(f"kn{i}", "a", "a") for i in range(4)]
    jobs += [(f"v{t}", "a", "a") for t in range(2)]
    jobs += [(f"xk{i}", "a", "a") for i in range(2)]
    jobs += [(f"qT{i}", "a", "a") for i in range(4)]
    jobs += [(f"s0{i}", "v", "v") for i in range(2)]
    jobs += [(f"s1{i}", "v", "v") for i in range(4)]
    jobs += [(f"xk{i}", "a", "a") for i in range(2, 4)]
    jobs += [(f"pT0{i}", "a", "a") for i in range(2)]
    jobs += [(f"pT1{i}", "a", "a") for i in range(4)]
    jobs += [(f"o{t}", "v", "v") for t in range(2)]
    jobs += [(f"xv{i}", "a", "a") for i in range(2)]
    jobs += [(f"oT{t}", "v", "v") for t in range(2)]
    jobs += [(f"xv{i}", "a", "a") for i in range(2, 4)]
    jobs += [("mean", "v", "v"), ("var", "a", "v")]
    jobs += [(f"w{t}{n}", "v", "v") for t in range(2) for n in range(2)]
    jobs += [(f"h2T{i}", "v", "v") for i in range(4)]
    jobs += [(f"xq{i}", "a", "a") for i in range(4)]
    jobs += [(f"xs{t}{g}", "v", "v") for t in range(2) for g in range(2)]
    jobs += [(f"xp{t}{g}", "a", "a") for t in range(2) for g in range(2)]
    jobs += [(f"xo{i}", "a", "a") for i in range(4)]
    jobs += [(f"wo{t}{n}", "v", "v") for t in range(2) for n in range(2)]
    jobs += [(f"tT{i}", "v", "v") for i in range(4)]
    jobs += [("logits", "v", "v"), ("rank", "v", "v"), ("count", "v", "v"), ("meta", "v", "v"), ("gT", "v", "v")]
    jobs += [(f"bd{t}{n}", "v", "v") for t in range(2) for n in range(2)]
    return jobs


def build_program(nc, x, mem, positions, g_mix, w_in, g_q, w_uq, g_kv, w_ukv, w_dw, b_dw, g_conv_ln,
                  b_conv_ln, w_out, g_xattn, g_mem, w_xq, w_xkv, w_xo, g_ffn, w_router, b_router,
                  w_up, b_up, w_down, b_down, g_final, out):
    fp32, i32, u32 = mybir.dt.float32, mybir.dt.int32, mybir.dt.uint32
    ALU = mybir.AluOpType
    ACT = mybir.ActivationFunctionType
    AX = mybir.AxisListType

    ctx = ExitStack()
    with ctx:
        def sb(name, cols, dt=fp32):
            return ctx.enter_context(nc.sbuf_tensor(name, [P, cols], dt))

        def sem(name):
            return ctx.enter_context(nc.semaphore(name))

        ring = sb("ring", 20 * SLAB)

        def slab(i, n=1):
            return ring[:, i * SLAB:(i + n) * SLAB]

        def carve(base, sizes):
            found = {}
            for name, n in sizes:
                found[name] = (base, n)
                base += n
            return found, base

        w_in_sb = ring[:, 0:KT * IN_COLS].rearrange("p (k n) -> p k n", k=KT)
        low, end = carve(KT * IN_COLS, [
            ("uq", 2 * HEADS * QK), ("ukv", HEADS * (NOPE + VDIM)), ("cqT", 2 * T), ("ckvT", T),
            ("krow", TT * QK), ("mask", TT * T), ("vrow1", P), ("vrow2", P), ("sg", 2 * T), ("trig", 2 * TT * 16)])
        assert end <= 8 * SLAB
        high, end = carve(8 * SLAB, [
            ("u", TT * TOK_COLS), ("qtok", TT * HEADS * QK), ("KT", HEADS * T), ("qT", HEADS * T),
            ("V", TT * HEADS * VDIM), ("S0", HEADS * P), ("S1", HEADS * T), ("PT0", HEADS * P),
            ("PT1", HEADS * T), ("z", CT * (TAPS - 1 + T)), ("acc", CT * T),
            ("freq", 16), ("pos", 2 * TT)])
        assert end <= 16 * SLAB

        def part(name):
            base, n = low[name] if name in low else high[name]
            return ring[:, base:base + n]

        uq_sb = part("uq").rearrange("p (k n) -> p k n", k=2)
        ukv_sb = part("ukv").rearrange("p (h n) -> p h n", h=HEADS)
        cqT = part("cqT").rearrange("p (k t) -> p k t", k=2)
        ckvT = part("ckvT")
        krow = part("krow").rearrange("p (a n) -> p a n", a=TT)
        mask = part("mask").rearrange("p (a k) -> p a k", a=TT)
        vrow1, vrow2 = part("vrow1"), part("vrow2")
        sg = part("sg").rearrange("p (a t) -> p a t", a=2)
        trig = part("trig").rearrange("p (f a j) -> p f a j", f=2, a=TT)
        u_tok = part("u").rearrange("p (a n) -> p a n", a=TT)
        q_tok = part("qtok").rearrange("p (a h n) -> p a h n", a=TT, h=HEADS)
        KTs = part("KT").rearrange("p (h t) -> p h t", h=HEADS)
        qTs = part("qT").rearrange("p (h t) -> p h t", h=HEADS)
        Vs = part("V").rearrange("p (a n) -> p a n", a=TT)
        S0 = part("S0").rearrange("p (h k) -> p h k", h=HEADS)
        S1 = part("S1").rearrange("p (h k) -> p h k", h=HEADS)
        PT0 = part("PT0").rearrange("p (h q) -> p h q", h=HEADS)
        PT1 = part("PT1").rearrange("p (h a q) -> p h a q", h=HEADS, a=TT)
        z = part("z").rearrange("p (c t) -> p c t", c=CT)
        acc = part("acc").rearrange("p (c t) -> p c t", c=CT)
        o_tok = part("S0").rearrange("p (a n) -> p a n", a=TT)
        rtmp = part("S1")[:, 0:4 * HEADS * 16].rearrange("p (i h j) -> p i h j", i=4, h=HEADS)
        ktmp = part("S1")[:, 512:512 + 4 * TT * 16].rearrange("p (i a j) -> p i a j", i=4, a=TT)
        ttmp = part("S0")[:, 0:8 * TT * 16].rearrange("p (i a j) -> p i a j", i=8, a=TT)
        sq4 = part("qtok")[:, 0:CT * T].rearrange("p (c t) -> p c t", c=CT)
        rstd_t = part("u")[:, 0:T]
        px = slab(13).rearrange("p (a h m) -> p a h m", a=TT, h=XH)
        ptx = slab(14).rearrange("p (h a q) -> p h a q", h=XH, a=M // P)
        x1n = slab(15).rearrange("p (a k q) -> p a k q", a=TT, k=KT)
        wk_sb = slab(16, 4).rearrange("p (k n) -> p k n", k=KT)
        wout_sb = slab(16, 4).rearrange("p (k n) -> p k n", k=KT)
        wv_sb = slab(0, 4).rearrange("p (k n) -> p k n", k=KT)
        wxq_sb = slab(4, 4).rearrange("p (k n) -> p k n", k=KT)
        wxo_sb = slab(0, 4).rearrange("p (k n) -> p k n", k=KT)

        buf_x = sb("buf_x", TT * D)
        buf_f = sb("buf_f", KT * T)
        buf_m = sb("buf_m", KT * T)
        buf_k = sb("buf_k", KT * T)
        buf_v = sb("buf_v", TT * D)
        xs = buf_x[:, :].rearrange("p (a n) -> p a n", a=TT)
        hT = buf_f[:, :].rearrange("p (k t) -> p k t", k=KT)
        yT = hT
        qT2 = hT
        tT = hT
        mT = buf_m[:, :].rearrange("p (k t) -> p k t", k=KT)
        h2T = mT
        oT2 = mT
        mem_sb = buf_k[:, :].rearrange("p (a n) -> p a n", a=TT)
        kTm = buf_k[:, :].rearrange("p (k m) -> p k m", k=KT)
        rows = buf_k[:, :].rearrange("p (a k q) -> p a k q", a=TT, k=KT)
        xn = buf_v[:, :].rearrange("p (a k q) -> p a k q", a=TT, k=KT)
        vm = buf_v[:, :].rearrange("p (a n) -> p a n", a=TT)
        gfin = buf_v[:, 0:D]
        gffn = buf_f[:, D:2 * D]
        bdown_sb = buf_v[:, D:2 * D]
        memn = part("PT1").rearrange("p (a k q) -> p a k q", a=TT, k=KT)

        ident = sb("ident", P)
        ones = sb("ones", P)
        mean_w = sb("mean_w", P)
        before = sb("before", P)
        slot_row = sb("slot_row", P)
        e_row = sb("e_row", E)
        sel32 = sb("sel32", 2 * E)
        wr_sb = sb("wr_sb", KT * E)
        br_sb = sb("br_sb", E)
        bup_sb = sb("bup_sb", E * 2 * KT)
        taps = sb("taps", TAPS * CT)
        vecs = sb("vecs", 15)
        gmix_sb = sb("gmix_sb", KT)
        gx_sb = sb("gx_sb", KT)
        gm_sb = sb("gm_sb", KT)
        stat = sb("stat", 48)
        roots = sb("roots", 14)
        newton = sb("newton", 2)
        eps = sb("eps", 1)
        freq = part("freq")
        pos_i = part("pos")[:, 0:TT].bitcast(i32)
        pos_f = part("pos")[:, TT:2 * TT]
        table = sb("table", E * 4)
        meta_i = sb("meta_i", 2 * E, i32)
        cols = buf_v[:, D + 260:D + 264]
        passed = buf_v[:, D + 800:D + 804]
        cap_row = buf_v[:, D + 804:D + 808]
        bcol = buf_v[:, D + 264:D + 280]
        P2 = buf_v[:, D:D + TT * P]
        PT2 = wr_sb
        gslot = buf_v[:, D + 256:D + 257]
        G_sb = buf_v[:, D + 288:D + 800]
        wr3 = wr_sb[:, :].rearrange("p (k e) -> p k e", k=KT)
        tab4 = table[:, :].rearrange("p (e c) -> p e c", c=4)
        bup4 = bup_sb[:, :].rearrange("p (e h j) -> p e h j", e=E, h=2)
        bcol2 = bcol.rearrange("p (h j) -> p h j", h=2)
        P2v = P2.rearrange("p (a s) -> p a s", a=TT)
        U_sb = buf_f[:, 0:1024].rearrange("p (j q) -> p j q", j=KT)
        A_sb = buf_f[:, 1024:2048].rearrange("p (j h t) -> p j h t", j=KT, h=2)
        xg = buf_m[:, 0:512].rearrange("p (k s) -> p k s", k=KT)
        scrap = buf_v[:, D + 280:D + 281]
        sig = buf_m[:, 512:1024].rearrange("p (j t) -> p j t", j=KT)
        actT = buf_m[:, 1024:1536].rearrange("p (j t) -> p j t", j=KT)
        y_sb = buf_m[:, 1536:2048]
        COMBINE = (6, 7, 4, 5)
        rt = buf_m

        banks = [ctx.enter_context(nc.psum_tensor(f"bank{i}", [P, BANK], fp32)) for i in range(8)]

        full = {"v": sem("psum_full_for_vector"), "a": sem("psum_full_for_scalar")}
        drained = {"v": sem("psum_drained_by_vector"), "a": sem("psum_drained_by_scalar")}
        JOBS = trunk_jobs()
        job_at = {name: i for i, (name, _, _) in enumerate(JOBS)}
        full_at, drained_at = {}, {}
        for name, first, last in JOBS:
            full_at[name] = (first, 1 + sum(1 for n, f, _ in JOBS[:job_at[name]] if f == first))
            drained_at[name] = (last, 1 + sum(1 for n, _, l in JOBS[:job_at[name]] if l == last))
        NDRAIN = {s: sum(1 for j in JOBS if j[2] == s) for s in "va"}

        def bank_of(job):
            return banks[job_at[job] % 8]

        def wait_full(eng, job):
            eng.wait_ge(full[full_at[job][0]], full_at[job][1])

        def wait_drained(eng, job):
            eng.wait_ge(drained[drained_at[job][0]], drained_at[job][1])

        names = ["x0", "x1", "mem", "pos", "vrow1", "vrow2", "gains", "win0", "win1", "win2", "win3", "uq", "ukv", "wk0",
                 "wk1", "wv", "wout", "wxq", "wxo", "router", "bup", "gffn", "late"]
        loaded = {n: sem(f"loaded_{n}") for n in names}
        const_ready = sem("const_ready")
        v_chain = sem("vector_step")
        conv_step = sem("conv_step")
        a_chain = sem("scalar_step")
        x_squares = sem("x_squares_summed")
        m_squares = sem("mem_squares_summed")
        xn_ready = sem("normed_x_ready")
        memn_ready = sem("normed_mem_ready")
        root_ready = sem("root_mean_square_ready")
        ROOTS = ["x", "mem", "cq", "ckv", "var", "x1", "x2", "out"]

        def wait_root(eng, name):
            eng.wait_ge(root_ready, 1 + ROOTS.index(name))

        trig_arg = sem("angles_ready")
        trig_ready = sem("cos_sin_ready")
        cq_squares = sem("latent_squares_summed")
        cq_ready = sem("normed_latents_ready")
        krow_ready = sem("rotated_key_ready")
        gate_sig = sem("conv_gate_sigmoid_ready")
        q_ready = sem("rotated_q_ready")
        s_ready = sem("mla_scores_ready")
        e_ready = sem("mla_exp_ready")
        zsq_ready = sem("conv_squares_ready")
        ln_ready = sem("conv_layernorm_ready")
        lnsig_ready = sem("conv_swish_sigmoid_ready")
        yconv_ready = sem("conv_output_ready")
        x1_squares = sem("x1_squares_summed")
        x1n_ready = sem("normed_x1_ready")
        xe_ready = sem("cross_exp_ready")
        px_ready = sem("cross_probs_ready")
        x2_squares = sem("x2_squares_summed")
        rows_ready = sem("expert_rows_ready")
        top_ready = sem("top_values_ready")
        topexp_ready = sem("top_exp_ready")
        picks_ready = sem("picks_and_gates_ready")
        slab_in = [sem(f"slab{i}_in") for i in range(20)]
        p2_ready = sem("onehot_ready")
        pt_full = sem("transposed_onehot_full")
        pt_copied = sem("transposed_onehot_copied")
        g_full = sem("gathered_rows_full")
        g_copied = sem("gathered_rows_copied")
        x_full = sem("gathered_columns_full")
        xg_ready = sem("gathered_columns_ready")
        up_steps = sem("up_slabs_used")
        u_by_a = sem("up_drained_by_scalar")
        u_by_v = sem("up_drained_by_vector")
        t_full = sem("up_transposed_full")
        biased = sem("up_biased")
        glu_ready = sem("glu_ready")
        lin_ready = sem("lin_ready")
        prod_ready = sem("glu_lin_ready")
        sig_ready = sem("glu_sigmoid_ready")
        act_ready = sem("act_ready")
        down_steps = sem("down_slabs_used")
        y_ready = sem("y_scaled_ready")
        c_full = sem("combined_full")
        y_added = sem("y_added")
        cols_ready = sem("expert_columns_ready")
        passed_ready = sem("passed_ranks_ready")
        bcol_ready = sem("expert_bias_ready")
        zeroed = sem("first_combine_zeroed")
        fin_squares = sem("final_squares_summed")
        fin_ready = sem("output_ready")
        stored = sem("output_stored")

        block = ctx.enter_context(nc.Block())

        pk = "(p k) n -> p k n"
        up_v = w_up[0].rearrange("e (p k) n -> e p k n", k=KT)
        down_v = w_down[0].rearrange("e (p k) n -> e p (k n)", k=KT)

        def krowsq(i):
            return part("PT0")[:, i * T:(i + 1) * T]

        @block.sync
        def _(sp):
            sp.dma_start(xs[:, 0, :], x[0, 0:P, :]).then_inc(loaded["x0"], 16)
            sp.dma_start(xs[:, 1, :], x[0, P:T, :]).then_inc(loaded["x1"], 16)
            for g, dst in ((g_mix, gmix_sb), (g_mem, gm_sb), (g_xattn, gx_sb)):
                sp.dma_start(dst[:, :], g[0].rearrange("(p k) -> p k", k=KT)).then_inc(loaded["gains"], 16)
            w_in_v = w_in[0].rearrange(pk, k=KT)
            for i in range(4):
                sp.dma_start(w_in_sb[:, 2 * i:2 * i + 2, :], w_in_v[:, 2 * i:2 * i + 2, :]).then_inc(loaded[f"win{i}"], 16)
            sp.dma_start(mem_sb, mem[0].rearrange("(a p) n -> p a n", p=P)).then_inc(loaded["mem"], 16)
            sp.dma_start(vrow1[0:TAPS * CT, :], w_dw[0].rearrange("w (c p) -> (w c) p", p=P)).then_inc(loaded["vrow1"], 16)
            at = 0
            for v, n in ((b_dw, CT), (g_conv_ln, CT), (b_conv_ln, CT), (g_q, 2), (g_kv, 1)):
                sp.dma_start(vrow2[at:at + n, :], v[0].rearrange("(c p) -> c p", p=P)).then_inc(loaded["vrow2"], 16)
                at += n
            sp.dma_start(pos_i, positions[0].rearrange("(a p) -> p a", p=P), allow_slow_non_contiguous=True).then_inc(loaded["pos"], 16)
            sp.dma_start(uq_sb, w_uq[0].rearrange("(k p) n -> p k n", p=P)).then_inc(loaded["uq"], 16)
            sp.dma_start(ukv_sb, w_ukv[0].rearrange("p (h n) -> p h n", h=HEADS)).then_inc(loaded["ukv"], 16)
            w_xkv_v = w_xkv[0].rearrange(pk, k=KT)
            for i in range(2):
                sp.dma_start(wk_sb[:, 4 * i:4 * i + 4, :], w_xkv_v[:, 4 * i:4 * i + 4, 0:D]).then_inc(loaded[f"wk{i}"], 16)
            sp.dma_start(wr3, w_router[0].rearrange(pk, k=KT)).then_inc(loaded["router"], 16)
            sp.dma_start(br_sb[:, :], b_router[0:1, :].broadcast_to([P, E])).then_inc(loaded["router"], 16)
            wait_drained(sp, "cv3")
            sp.dma_start(wv_sb, w_xkv_v[:, :, D:2 * D]).then_inc(loaded["wv"], 16)
            bup_v = b_up[0].rearrange("e (h p j) -> p e h j", h=2, j=KT)
            for h in range(2):
                sp.dma_start(bup4[:, :, h, :], bup_v[:, :, h, :]).then_inc(loaded["bup"], 16)
            wait_drained(sp, "xk3")
            sp.dma_start(wout_sb, w_out[0].rearrange("(k p) n -> p k n", p=P)).then_inc(loaded["wout"], 16)
            wait_drained(sp, "s13")
            sp.dma_start(wxq_sb, w_xq[0].rearrange(pk, k=KT)).then_inc(loaded["wxq"], 16)
            wait_drained(sp, "xv3")
            sp.dma_start(wxo_sb, w_xo[0].rearrange("(k p) n -> p k n", p=P)).then_inc(loaded["wxo"], 16)

            def load_up(e, base, ks):
                for k in ks:
                    sp.dma_start(slab(base + k), up_v[e, :, k, :]).then_inc(slab_in[base + k], 16)

            def load_down(e):
                for s in range(4):
                    sp.dma_start(slab(16 + s), down_v[e, :, s * SLAB:(s + 1) * SLAB]).then_inc(slab_in[16 + s], 16)

            wait_drained(sp, "oT1")
            sp.wait_ge(yconv_ready, 1)
            load_up(0, 8, range(0, 5))
            wait_drained(sp, "w11")
            load_down(0)
            wait_drained(sp, "xq3")
            load_up(1, 0, range(4, 8))
            wait_drained(sp, "xs11")
            sp.dma_start(gffn, g_ffn[0:1, :].broadcast_to([P, D])).then_inc(loaded["gffn"], 16)
            wait_drained(sp, "xo3")
            load_up(0, 8, range(5, 8))
            sp.dma_start(gfin, g_final.rearrange("(a n) -> a n", a=1).broadcast_to([P, D])).then_inc(loaded["late"], 16)
            sp.dma_start(bdown_sb[0:E, :], b_down[0]).then_inc(loaded["late"], 16)
            wait_drained(sp, "wo11")
            load_up(1, 0, range(0, 4))

            wait_drained(sp, "meta")

            def last_block(e):
                extra = sp.value_load(meta_i[0:1, bass.ds(e, 1)], min_val=0, max_val=T // CAP - 1)
                first = sp.value_load(meta_i[0:1, bass.ds(e + E, 1)], min_val=0, max_val=E + T * TOPK // CAP)
                return sp.snap(first + extra)

            def replace_up(e, n, base):
                for k in range(KT):
                    sp.wait_ge(up_steps, n * KT + (k + 1))
                    load_up(e, base, [k])

            def replace_down(e, n):
                for s in range(4):
                    sp.wait_ge(down_steps, n * 4 + (s + 1))
                    sp.dma_start(slab(16 + s), down_v[e, :, s * SLAB:(s + 1) * SLAB]).then_inc(slab_in[16 + s], 16)

            with sp.Fori(0, E // 2 - 1) as pair:
                e = pair * 2
                n = last_block(e)
                replace_up(e + 2, n, 8)
                replace_down(e + 1, n)
                n = last_block(e + 1)
                replace_up(e + 3, n, 0)
                replace_down(e + 2, n)
            replace_down(E - 1, last_block(E - 2))
            for a in range(TT):
                sp.wait_ge(fin_ready, a + 1)
                sp.dma_start(out[0, a * P:(a + 1) * P, :], xs[:, a, :]).then_inc(stored, 16)
            sp.wait_ge(stored, 16 * TT)

        @block.gpsimd
        def _(pool):
            g = nc.gpsimd
            steps = [0]

            def done(ins):
                steps[0] += 1
                ins.then_inc(const_ready, 1)
                pool.wait_ge(const_ready, steps[0])

            for j in range(16):
                done(g.memset(freq[:, j:j + 1], float(np.float32(ROPE_THETA) ** np.float32(-2.0 * j / ROPE))))
            done(g.memset(eps[:, :], EPS))
            done(g.memset(ident[:, :], 0.0))
            done(g.affine_select(out=ident[:, :], in_=ident[:, :], compare_op=ALU.not_equal, fill=1.0,
                                 base=0, pattern=[[-1, P]], channel_multiplier=1))
            done(g.memset(ones[:, :], 1.0))
            done(g.memset(mean_w[:, :], 1.0 / CONV))
            done(g.affine_select(out=before[:, :], in_=ones[:, :], compare_op=ALU.is_gt, fill=0.0,
                                 base=0, pattern=[[1, P]], channel_multiplier=-1))
            done(g.affine_select(out=sel32[0:E, E:2 * E], in_=ones[0:E, 0:E], compare_op=ALU.is_gt, fill=0.0,
                                 base=0, pattern=[[1, E]], channel_multiplier=-1))
            done(g.tensor_copy(sel32[0:E, 0:E], ident[0:E, 0:E]))
            done(g.iota(slot_row[:, :], pattern=[[0, 2], [1, CAP]], base=0, channel_multiplier=0,
                        allow_small_or_imprecise_dtypes=True))
            done(g.iota(e_row[:, :], pattern=[[1, E]], base=0, channel_multiplier=0,
                        allow_small_or_imprecise_dtypes=True))
            done(g.memset(mask, 0.0))
            for a in range(TT):
                for c in range(P // CHUNK):
                    seen = a * P + (c + 1) * CHUNK
                    if seen < T:
                        done(g.memset(mask[c * CHUNK:(c + 1) * CHUNK, a, seen:T], MASKED))
            done(g.memset(krow, 0.0))
            done(g.memset(z[:, :, 0:TAPS - 1], 0.0))

            wait_drained(pool, "wo11")
            wait_drained(pool, "bd11")
            g.memset(y_sb, 0.0).then_inc(zeroed, 1)
            g.memset(PT2[:, :], 0.0).then_inc(zeroed, 1)
            g.memset(cap_row[:, 0:TT], float(CAP)).then_inc(zeroed, 1)
            g.memset(cap_row[:, TT:], 0.0).then_inc(zeroed, 1)
            pool.wait_ge(zeroed, 4)

            with pool.Fori(0, E) as e:
                extra = pool.value_load(meta_i[0:1, bass.ds(e, 1)], min_val=0, max_val=T // CAP - 1)
                first = pool.value_load(meta_i[0:1, bass.ds(e + E, 1)], min_val=0, max_val=E + T * TOPK // CAP)
                pool.wait_ge(cols_ready, first)
                pool.wait_ge(passed_ready, first + e)
                g.tensor_tensor(passed, cap_row, cap_row, ALU.subtract).then_inc(passed_ready, 1)
                with pool.Fori(0, pool.snap(extra + 1)) as r:
                    b = pool.snap(first + r)
                    pool.wait_ge(pt_full, b)
                    pool.wait_ge(passed_ready, e + b + 1)
                    g.tensor_tensor(cols, table[:, bass.ds(e * 4, 4)], passed, ALU.subtract).then_inc(cols_ready, 1)
                    pool.wait_ge(cols_ready, b + 1)
                    g.tensor_tensor(passed, passed, cap_row, ALU.add).then_inc(passed_ready, 1)
            last_b = pool.value_load(meta_i[0:1, 2 * E - 1:2 * E], min_val=0, max_val=E + T * TOPK // CAP)
            last_r = pool.value_load(meta_i[0:1, E - 1:E], min_val=0, max_val=T // CAP - 1)
            blocks = pool.snap(last_b + last_r + 1)
            pool.wait_ge(pt_full, blocks)
            pool.wait_ge(passed_ready, blocks + E)
            g.tensor_tensor(cols, passed, cap_row, ALU.add).then_inc(cols_ready, 1)

        N_CONST = 9 + 17 + 1 + 3 + 2

        @block.scalar
        def _(act):
            a = nc.scalar
            chain = [0]

            def link(ins):
                chain[0] += 1
                ins.then_inc(a_chain, 1)
                act.wait_ge(a_chain, chain[0])

            def root(dst, src, n):
                a.activation(dst, src, ACT.Sqrt, bias=eps[:, 0:1], scale=1.0 / n).then_inc(root_ready, 1)

            def drain(job, ins):
                ins.then_inc(drained["a"], 1)

            for i in range(TT):
                act.wait_ge(loaded[f"x{i}"], 16)
                a.activation(xn[:, i].rearrange("p k q -> p (k q)"), xs[:, i, :], ACT.Square,
                             accum_out=stat[:, i:i + 1]).then_inc(x_squares, 1)
            act.wait_ge(x_squares, TT)
            act.wait_ge(const_ready, 17)
            root(roots[:, 0:2], stat[:, 0:2], D)
            act.wait_ge(loaded["mem"], 16)
            for i in range(TT):
                a.activation(memn[:, i].rearrange("p k q -> p (k q)"), mem_sb[:, i, :], ACT.Square,
                             accum_out=stat[:, 2 + i:3 + i]).then_inc(m_squares, 1)
            act.wait_ge(m_squares, TT)
            root(roots[:, 2:4], stat[:, 2:4], D)
            act.wait_ge(trig_arg, 2)
            a.activation(trig, ttmp[:, 2:4], ACT.Sin).then_inc(trig_ready, 1)
            wait_drained(act, "u1")
            for i in range(TT):
                a.activation(krowsq(i), u_tok[:, i, 0:Q_LORA], ACT.Square,
                             accum_out=stat[:, 4 + i:5 + i]).then_inc(cq_squares, 1)
            for i in range(TT):
                a.activation(krowsq(2 + i)[:, 0:KV_LORA], u_tok[:, i, Q_LORA:Q_LORA + KV_LORA], ACT.Square,
                             accum_out=stat[:, 6 + i:7 + i]).then_inc(cq_squares, 1)
            act.wait_ge(cq_squares, 4)
            root(roots[:, 4:6], stat[:, 4:6], Q_LORA)
            root(roots[:, 6:8], stat[:, 6:8], KV_LORA)
            act.wait_ge(loaded["gains"], 48)
            for i in range(4):
                job = f"mT{i}"
                wait_full(act, job)
                b = bank_of(job)
                link(a.activation(mT[:, 2 * i, :], b[:, 0:T], ACT.Copy, scale=gm_sb[:, 2 * i:2 * i + 1]))
                drain(job, a.activation(mT[:, 2 * i + 1, :], b[:, T:2 * T], ACT.Copy,
                                        scale=gm_sb[:, 2 * i + 1:2 * i + 2]))
            for c in range(CT):
                job = f"cv{c}"
                wait_full(act, job)
                if c >= 2:
                    wait_drained(act, f"cv{c - 2}")
                a.activation(sg[:, c % 2, :], bank_of(job)[:, T:2 * T], ACT.Sigmoid).then_inc(gate_sig, 1)
            wait_full(act, "krT")
            drain("krT", a.activation(KTs[NOPE:QK, :, :],
                                      bank_of("krT")[NOPE:QK, 0:T].unsqueeze(1).broadcast_to([ROPE, HEADS, T]), ACT.Copy))
            for t in range(TT):
                for h in range(2):
                    job = f"q{t}{h}"
                    wait_full(act, job)
                    drain(job, a.activation(q_tok[:, t, 4 * h:4 * h + 4, :].rearrange("p h n -> p (h n)"),
                                            bank_of(job)[:, 0:4 * QK], ACT.Copy))
            for i in range(4):
                job = f"kn{i}"
                wait_full(act, job)
                drain(job, a.activation(KTs[0:NOPE, 2 * i:2 * i + 2, :].rearrange("p h t -> p (h t)"),
                                        bank_of(job)[0:NOPE, :], ACT.Copy))
            for t in range(TT):
                job = f"v{t}"
                wait_full(act, job)
                drain(job, a.activation(Vs[:, t, :], bank_of(job)[:, :], ACT.Copy))

            def key_job(i):
                job = f"xk{i}"
                wait_full(act, job)
                drain(job, a.activation(kTm[:, 2 * i:2 * i + 2, :].rearrange("p k m -> p (k m)"),
                                        bank_of(job)[:, :], ACT.Copy))

            key_job(0)
            key_job(1)
            for i in range(4):
                job = f"qT{i}"
                wait_full(act, job)
                drain(job, a.activation(qTs[0:QK, 2 * i:2 * i + 2, :].rearrange("p h t -> p (h t)"),
                                        bank_of(job)[0:QK, :], ACT.Copy))
            act.wait_ge(s_ready, 1)
            a.activation(part("S0"), part("S0"), ACT.Exp, scale=float(QK) ** -0.5).then_inc(e_ready, 1)
            act.wait_ge(s_ready, 2)
            a.activation(part("S1"), part("S1"), ACT.Exp, scale=float(QK) ** -0.5).then_inc(e_ready, 1)
            key_job(2)
            key_job(3)
            for i in range(2):
                job = f"pT0{i}"
                wait_full(act, job)
                drain(job, a.activation(PT0[:, 4 * i:4 * i + 4, :].rearrange("p h q -> p (h q)"),
                                        bank_of(job)[:, :], ACT.Copy))
            for i in range(4):
                job = f"pT1{i}"
                wait_full(act, job)
                drain(job, a.activation(PT1[:, 2 * i:2 * i + 2].rearrange("p h a q -> p (h a q)"),
                                        bank_of(job)[:, :], ACT.Copy))
            for i in range(2):
                job = f"xv{i}"
                wait_full(act, job)
                drain(job, a.activation(vm[:, 0, i * BANK:(i + 1) * BANK], bank_of(job)[:, :], ACT.Copy))
            for i in range(2):
                job = f"xv{2 + i}"
                wait_full(act, job)
                drain(job, a.activation(vm[:, 1, i * BANK:(i + 1) * BANK], bank_of(job)[:, :], ACT.Copy))
            wait_drained(act, "mean")
            a.activation(sq4, acc, ACT.Square).then_inc(zsq_ready, 1)
            wait_full(act, "var")
            root(rstd_t, bank_of("var")[:, 0:T], 1)
            act.wait_ge(ln_ready, CT)
            a.activation(sq4, acc, ACT.Sigmoid).then_inc(lnsig_ready, 1)
            for t in range(TT):
                wait_drained(act, f"w{t}1")
                a.activation(x1n[:, t].rearrange("p k q -> p (k q)"), xs[:, t, :], ACT.Square,
                             accum_out=stat[:, 8 + t:9 + t]).then_inc(x1_squares, 1)
            act.wait_ge(x1_squares, TT)
            root(roots[:, 8:10], stat[:, 8:10], D)
            for i in range(4):
                job = f"xq{i}"
                wait_full(act, job)
                drain(job, a.activation(qT2[:, 2 * i:2 * i + 2, :].rearrange("p k t -> p (k t)"),
                                        bank_of(job)[:, :], ACT.Copy))
            for t in range(TT):
                wait_drained(act, f"xs{t}1")
                v = px[:, t].rearrange("p h m -> p (h m)")
                a.activation(v, v, ACT.Exp, scale=float(XD) ** -0.5).then_inc(xe_ready, 1)
            for t in range(TT):
                for g in range(2):
                    job = f"xp{t}{g}"
                    wait_full(act, job)
                    drain(job, a.activation(ptx[:, 2 * g:2 * g + 2, :, t * P:(t + 1) * P],
                                            bank_of(job)[:, :].rearrange("p (h a q) -> p h a q", h=2, a=2), ACT.Copy))
            for i in range(4):
                job = f"xo{i}"
                wait_full(act, job)
                drain(job, a.activation(oT2[:, 2 * i:2 * i + 2, :].rearrange("p k t -> p (k t)"),
                                        bank_of(job)[:, :], ACT.Copy))
            for t in range(TT):
                wait_drained(act, f"wo{t}1")
                a.activation(rows[:, t].rearrange("p k q -> p (k q)"), xs[:, t, :], ACT.Square,
                             accum_out=stat[:, 10 + t:11 + t]).then_inc(x2_squares, 1)
            act.wait_ge(x2_squares, TT)
            root(roots[:, 10:12], stat[:, 10:12], D)
            act.wait_ge(top_ready, 1)
            a.activation(stat[:, 16:16 + TT * TOPK], stat[:, 16:16 + TT * TOPK], ACT.Exp).then_inc(topexp_ready, 1)

            wait_drained(act, "meta")
            wait_drained(act, "bd11")

            def gathered(b):
                act.wait_ge(g_full, b + 1)
                a.activation(G_sb, banks[4][:, :], ACT.Copy).then_inc(g_copied, 1)

            def gathered_columns(b):
                act.wait_ge(x_full, b + 1)
                a.activation(xg.rearrange("p (h c) s -> p c h s", h=2),
                             banks[2][:, :].rearrange("p (c h s) -> p c h s", c=4, h=2), ACT.Copy).then_inc(xg_ready, 1)

            gathered(0)
            gathered_columns(0)
            with act.Fori(0, E) as e:
                extra = act.value_load(meta_i[0:1, bass.ds(e, 1)], min_val=0, max_val=T // CAP - 1)
                first = act.value_load(meta_i[0:1, bass.ds(e + E, 1)], min_val=0, max_val=E + T * TOPK // CAP)
                with act.Fori(0, act.snap(extra + 1)) as r:
                    b = act.snap(first + r)
                    a.activation(scrap, eps[:, 0:1], ACT.Sigmoid)
                    act.wait_ge(up_steps, b * KT + KT)
                    a.activation(U_sb[:, :, 0:64].rearrange("p j q -> p q j"),
                                 banks[0][:, :].rearrange("p (q j) -> p q j", j=KT), ACT.Copy).then_inc(u_by_a, 1)
                    for i in range(2):
                        act.wait_ge(glu_ready, b * 2 + (i + 1))
                        a.activation(sig[:, 4 * i:4 * i + 4, :], A_sb[:, 4 * i:4 * i + 4, 0, :], ACT.Sigmoid,
                                     scale=ALPHA).then_inc(sig_ready, 1)
                    act.wait_ge(pt_full, b + 1)
                    a.activation(PT2[:, :], banks[6][:, 0:T], ACT.Copy)
                    a.activation(gslot, banks[6][:, T:T + 1], ACT.Copy).then_inc(pt_copied, 1)
                    gathered(b + 1)
                    gathered_columns(b + 1)
                    act.wait_ge(down_steps, b * 4 + 4)
                    act.wait_ge(pt_copied, b + 1)
                    a.activation(y_sb, banks[5][:, :], ACT.Copy, scale=gslot).then_inc(y_ready, 1)
            last_b = act.value_load(meta_i[0:1, 2 * E - 1:2 * E], min_val=0, max_val=E + T * TOPK // CAP)
            last_r = act.value_load(meta_i[0:1, E - 1:E], min_val=0, max_val=T // CAP - 1)
            act.wait_ge(y_added, act.snap((last_b + last_r) * 4 + 8))
            for t in range(TT):
                a.activation(buf_f[:, t * D:(t + 1) * D], xs[:, t, :], ACT.Square,
                             accum_out=stat[:, 12 + t:13 + t]).then_inc(fin_squares, 1)
            act.wait_ge(fin_squares, TT)
            root(roots[:, 12:14], stat[:, 12:14], D)

        @block.vector
        def _(dve):
            v = nc.vector
            chain = [0]

            def link(ins):
                chain[0] += 1
                ins.then_inc(v_chain, 1)
                dve.wait_ge(v_chain, chain[0])

            def rstd(name, c, n):
                wait_root(dve, name)
                r, ms, q = roots[:, c:c + 2], stat[:, c:c + 2], newton[:, :]
                link(v.reciprocal(r, r))
                link(v.tensor_scalar(ms, ms, 1.0 / n, EPS, ALU.mult, ALU.add))
                link(v.tensor_tensor(q, r, r, ALU.mult))
                link(v.tensor_tensor(q, q, ms, ALU.mult))
                link(v.tensor_scalar(q, q, -0.5, 1.5, ALU.mult, ALU.add))
                link(v.tensor_tensor(ms, r, q, ALU.mult))

            def apart(dst, src, scale):
                return v.tensor_scalar(dst.rearrange("p k q -> p q k"), src.rearrange("p (q k) -> p q k", k=KT),
                                       scale, None, ALU.mult)

            def free(job, ins):
                ins.then_inc(drained["v"], 1)

            def bc(ap, n):
                return ap.unsqueeze(2).broadcast_to([ap.shape[0], ap.shape[1], n])

            rstd("x", 0, D)
            for t in range(TT):
                apart(xn[:, t], xs[:, t, :], stat[:, t:t + 1]).then_inc(xn_ready, 1)
            dve.wait_ge(loaded["pos"], 16)
            dve.wait_ge(const_ready, 16)
            link(v.tensor_copy(pos_f, pos_i))
            ang = ttmp[:, 0]
            for t in range(TT):
                link(v.tensor_scalar(ang[:, t, :], freq, pos_f[:, t:t + 1], None, ALU.mult))
            ROUND = 12582912.0
            two_pi = 2 * np.pi
            c1 = float(np.float32(6.28125))
            c2 = float(np.float32(np.round((two_pi - c1) * 2 ** 22) / 2 ** 22))
            c3 = float(two_pi - c1 - c2)
            for f, quarter in ((0, 0.25), (1, 0.0)):
                k, r = ttmp[:, 1], ttmp[:, 2 + f]
                link(v.tensor_scalar(k, ang, 1.0 / two_pi, quarter, ALU.mult, ALU.add))
                link(v.tensor_scalar(k, k, ROUND, None, ALU.add))
                link(v.tensor_scalar(k, k, ROUND, None, ALU.subtract))
                link(v.scalar_tensor_tensor(r, k, -c1, ang, ALU.mult, ALU.add))
                link(v.scalar_tensor_tensor(r, k, -c2, r, ALU.mult, ALU.add))
                link(v.scalar_tensor_tensor(r, k, -c3, r, ALU.mult, ALU.add))
                if f == 0:
                    link(v.tensor_scalar(r, r, float(np.pi / 2), None, ALU.add))
                v.tensor_scalar(r, r, 3.1415925, -3.1415925, ALU.min, ALU.max).then_inc(trig_arg, 1)
                dve.wait_ge(trig_arg, f + 1)
            dve.wait_ge(const_ready, N_CONST)
            wait_full(dve, "vec")
            b = bank_of("vec")
            link(v.tensor_copy(taps[:, :], b[:, 0:TAPS * CT]))
            free("vec", v.tensor_copy(vecs[:, :], b[:, P:P + 15]))
            dve.wait_ge(loaded["gains"], 48)
            for i in range(4):
                job = f"hT{i}"
                wait_full(dve, job)
                free(job, v.tensor_tensor(hT[:, 2 * i:2 * i + 2, :], bank_of(job)[:, :].rearrange("p (k t) -> p k t", k=2),
                                          bc(gmix_sb[:, 2 * i:2 * i + 2], T), ALU.mult))
            rstd("mem", 2, D)
            for t in range(TT):
                apart(memn[:, t], mem_sb[:, t, :], stat[:, 2 + t:3 + t]).then_inc(memn_ready, 1)
            for t in range(TT):
                wait_full(dve, f"u{t}")
                free(f"u{t}", v.tensor_copy(u_tok[:, t, :], bank_of(f"u{t}")[:, 0:TOK_COLS]))
            wait_drained(dve, "u1")
            dve.wait_ge(trig_ready, 1)

            def rotate(out1, out2, x1, x2, cos, sin, tmp):
                link(v.tensor_tensor(tmp[0], x1, cos, ALU.mult))
                link(v.tensor_tensor(tmp[1], x2, sin, ALU.mult))
                link(v.tensor_tensor(tmp[2], x1, sin, ALU.mult))
                link(v.tensor_tensor(tmp[3], x2, cos, ALU.mult))
                link(v.tensor_tensor(out1, tmp[0], tmp[1], ALU.subtract))
                return v.tensor_tensor(out2, tmp[2], tmp[3], ALU.add)

            o3 = Q_LORA + KV_LORA
            rotate(krow[:, :, NOPE:NOPE + 16], krow[:, :, NOPE + 16:QK], u_tok[:, :, o3:o3 + 16],
                   u_tok[:, :, o3 + 16:o3 + 32], trig[:, 0], trig[:, 1],
                   [ktmp[:, i] for i in range(4)]).then_inc(krow_ready, 1)
            rstd("cq", 4, Q_LORA)
            rstd("ckv", 6, KV_LORA)
            for t in range(TT):
                cq, ckv = u_tok[:, t, 0:Q_LORA], u_tok[:, t, Q_LORA:o3]
                v.tensor_scalar(cq, cq, stat[:, 4 + t:5 + t], None, ALU.mult).then_inc(cq_ready, 1)
                v.tensor_scalar(ckv, ckv, stat[:, 6 + t:7 + t], None, ALU.mult).then_inc(cq_ready, 1)
            for c in range(CT):
                dve.wait_ge(gate_sig, c + 1)
                free(f"cv{c}", v.tensor_tensor(z[:, c, TAPS - 1:], bank_of(f"cv{c}")[:, 0:T], sg[:, c % 2, :], ALU.mult))
            wait_full(dve, "cqT")
            free("cqT", v.tensor_tensor(cqT, bank_of("cqT")[:, :].rearrange("p (k t) -> p k t", k=2),
                                        bc(vecs[:, 12:14], T), ALU.mult))
            wait_full(dve, "ckvT")
            free("ckvT", v.tensor_scalar(ckvT, bank_of("ckvT")[:, 0:T], vecs[:, 14:15], None, ALU.mult))
            for t in range(TT):
                wait_drained(dve, f"q{t}1")
                cos = trig[:, 0, t, :].unsqueeze(1).broadcast_to([P, HEADS, 16])
                sin = trig[:, 1, t, :].unsqueeze(1).broadcast_to([P, HEADS, 16])
                x1, x2 = q_tok[:, t, :, NOPE:NOPE + 16], q_tok[:, t, :, NOPE + 16:QK]
                rotate(x1, x2, x1, x2, cos, sin, [rtmp[:, i] for i in range(4)]).then_inc(q_ready, 1)

            conv_n = [0]

            def conv_taps(ws):
                for w in ws:
                    for c in range(CT):
                        n = conv_n[0]
                        if n >= CT:
                            dve.wait_ge(conv_step, n - CT + 1)
                        src, wt = z[:, c, w:w + T], taps[:, w * CT + c:w * CT + c + 1]
                        if w == 0:
                            ins = v.tensor_scalar(acc[:, c, :], src, wt, vecs[:, c:c + 1], ALU.mult, ALU.add)
                        else:
                            ins = v.scalar_tensor_tensor(acc[:, c, :], src, wt, acc[:, c, :], ALU.mult, ALU.add)
                        ins.then_inc(conv_step, 1)
                        conv_n[0] += 1

            wait_drained(dve, "cv3")
            dve.wait_ge(cq_squares, 4)
            conv_taps(range(0, 12))
            mx, sm = stat[:, 24:32], stat[:, 32:48]
            for t, S, keys, per in ((0, S0, P, 4), (1, S1, T, 2)):
                for i in range(HEADS // per):
                    job = f"s{t}{i}"
                    wait_full(dve, job)
                    m = mask[:, t, 0:keys].unsqueeze(1).broadcast_to([P, per, keys])
                    free(job, v.tensor_tensor(S[:, per * i:per * i + per, :],
                                              bank_of(job)[:, :].rearrange("p (h k) -> p h k", h=per), m, ALU.add))
                wait_drained(dve, f"s{t}{HEADS // per - 1}")
                link(v.tensor_reduce(mx, S, AX.X, ALU.max))
                v.tensor_tensor(S, S, bc(mx, keys), ALU.subtract).then_inc(s_ready, 1)
            for t, S in ((0, S0), (1, S1)):
                dve.wait_ge(e_ready, t + 1)
                link(v.tensor_reduce(sm[:, 8 * t:8 * t + 8], S, AX.X, ALU.add))
            link(v.reciprocal(sm, sm))
            conv_taps(range(12, 22))
            for t in range(TT):
                wait_full(dve, f"o{t}")
                free(f"o{t}", v.tensor_tensor(o_tok[:, t, :].rearrange("p (h n) -> p h n", h=HEADS),
                                              bank_of(f"o{t}")[:, :].rearrange("p (h n) -> p h n", h=HEADS),
                                              bc(sm[:, 8 * t:8 * t + 8], VDIM), ALU.mult))
            for t in range(TT):
                wait_full(dve, f"oT{t}")
                free(f"oT{t}", v.tensor_copy(yT[:, 0:4, t * P:(t + 1) * P],
                                             bank_of(f"oT{t}")[:, :].rearrange("p (k q) -> p k q", k=4)))
            conv_taps(range(22, TAPS))
            dve.wait_ge(conv_step, conv_n[0])
            wait_full(dve, "mean")
            free("mean", v.tensor_tensor(acc, acc, bank_of("mean")[:, 0:T].unsqueeze(1).broadcast_to([P, CT, T]), ALU.subtract))
            wait_drained(dve, "mean")
            wait_root(dve, "var")
            link(v.reciprocal(rstd_t, rstd_t))
            q = part("PT0")[:, 0:T]
            link(v.tensor_tensor(q, rstd_t, rstd_t, ALU.mult))
            free("var", v.scalar_tensor_tensor(q, bank_of("var")[:, 0:T], EPS, q, ALU.add, ALU.mult))
            wait_drained(dve, "var")
            link(v.tensor_scalar(q, q, -0.5, 1.5, ALU.mult, ALU.add))
            link(v.tensor_tensor(rstd_t, rstd_t, q, ALU.mult))
            link(v.tensor_tensor(acc, acc, rstd_t.unsqueeze(1).broadcast_to([P, CT, T]), ALU.mult))
            for c in range(CT):
                v.tensor_scalar(acc[:, c, :], acc[:, c, :], vecs[:, 4 + c:5 + c], vecs[:, 8 + c:9 + c],
                                ALU.mult, ALU.add).then_inc(ln_ready, 1)
            dve.wait_ge(lnsig_ready, 1)
            v.tensor_tensor(yT[:, 4:8, :], acc, sq4, ALU.mult).then_inc(yconv_ready, 1)
            for t in range(TT):
                for n in range(2):
                    job = f"w{t}{n}"
                    wait_full(dve, job)
                    s = xs[:, t, n * BANK:(n + 1) * BANK]
                    free(job, v.tensor_tensor(s, bank_of(job)[:, :], s, ALU.add))
            rstd("x1", 8, D)
            for t in range(TT):
                apart(x1n[:, t], xs[:, t, :], stat[:, 8 + t:9 + t]).then_inc(x1n_ready, 1)
            for i in range(4):
                job = f"h2T{i}"
                wait_full(dve, job)
                free(job, v.tensor_tensor(h2T[:, 2 * i:2 * i + 2, :], bank_of(job)[:, :].rearrange("p (k t) -> p k t", k=2),
                                          bc(gx_sb[:, 2 * i:2 * i + 2], T), ALU.mult))
            for t in range(TT):
                for g in range(2):
                    job = f"xs{t}{g}"
                    wait_full(dve, job)
                    bk = bank_of(job)[:, :].rearrange("p (h m) -> p h m", h=2)
                    m2 = mx[:, 2 * g:2 * g + 2]
                    link(v.tensor_reduce(m2, bk, AX.X, ALU.max))
                    free(job, v.tensor_tensor(px[:, t, 2 * g:2 * g + 2, :], bk, bc(m2, M), ALU.subtract))
            for t in range(TT):
                dve.wait_ge(xe_ready, t + 1)
                s4 = sm[:, 4 * t:4 * t + 4]
                link(v.tensor_reduce(s4, px[:, t], AX.X, ALU.add))
                link(v.reciprocal(s4, s4))
                v.tensor_tensor(px[:, t], px[:, t], bc(s4, M), ALU.mult).then_inc(px_ready, 1)
            for t in range(TT):
                for n in range(2):
                    job = f"wo{t}{n}"
                    wait_full(dve, job)
                    s = xs[:, t, n * BANK:(n + 1) * BANK]
                    free(job, v.tensor_tensor(s, bank_of(job)[:, :], s, ALU.add))
            rstd("x2", 10, D)
            dve.wait_ge(loaded["gffn"], 16)
            for t in range(TT):
                v.scalar_tensor_tensor(rows[:, t].rearrange("p k q -> p q k"), xs[:, t, :].rearrange("p (q k) -> p q k", k=KT),
                                       stat[:, 10 + t:11 + t], gffn.rearrange("p (q k) -> p q k", k=KT),
                                       ALU.mult, ALU.mult).then_inc(rows_ready, 1)
            for i in range(4):
                job = f"tT{i}"
                wait_full(dve, job)
                free(job, v.tensor_copy(tT[:, 2 * i:2 * i + 2, :], bank_of(job)[:, :].rearrange("p (k t) -> p k t", k=2)))
            lg = rt[:, 0:2 * E].rearrange("p (a e) -> p a e", a=TT)
            pick = rt[:, 64:128].rearrange("p (a e) -> p a e", a=TT)
            gate = rt[:, 128:192].rearrange("p (a e) -> p a e", a=TT)
            top8 = rt[:, 192:208].rearrange("p (a j) -> p a j", a=TT)
            idx_u = rt[:, 208:224].bitcast(u32).rearrange("p (a j) -> p a j", a=TT)
            idx_f = rt[:, 224:240].rearrange("p (a j) -> p a j", a=TT)
            hit = rt[:, 240:304].rearrange("p (a e) -> p a e", a=TT)
            neg = rt[:, 304:306]
            tsum = rt[:, 306:308]
            count = rt[:, 308:309]
            rounds_c = rt[:, 309:310]
            step = rt[:, 310:311]
            gT_sb = rt[:, 320:320 + T]
            top4 = stat[:, 16:16 + TT * TOPK].rearrange("p (a j) -> p a j", a=TT)
            dve.wait_ge(loaded["router"], 32)
            wait_full(dve, "logits")
            free("logits", v.tensor_tensor(lg, bank_of("logits")[:, 0:2 * E].rearrange("p (a e) -> p a e", a=TT),
                                           br_sb[:, :].unsqueeze(1).broadcast_to([P, TT, E]), ALU.add))
            wait_drained(dve, "logits")
            for t in range(TT):
                link(v.max(top8[:, t, :], lg[:, t, :]))
                link(v.max_index(idx_u[:, t, :], top8[:, t, :], lg[:, t, :]))
            link(v.tensor_copy(idx_f, idx_u))
            for t in range(TT):
                ins = v.tensor_scalar(top4[:, t, :], top8[:, t, 0:TOPK], top8[:, t, 0:1], None, ALU.subtract)
                if t < TT - 1:
                    link(ins)
                else:
                    ins.then_inc(top_ready, 1)
            dve.wait_ge(topexp_ready, 1)
            link(v.tensor_reduce(tsum, top4, AX.X, ALU.add))
            link(v.reciprocal(tsum, tsum))
            link(v.tensor_tensor(top4, top4, bc(tsum, TOPK), ALU.mult))
            for t in range(TT):
                for j in range(TOPK):
                    link(v.tensor_scalar(hit[:, t, :], e_row[:, :], idx_f[:, t, j:j + 1], None, ALU.is_equal))
                    g1 = top4[:, t, j:j + 1]
                    if j == 0:
                        link(v.tensor_copy(pick[:, t, :], hit[:, t, :]))
                        ins = v.tensor_scalar(gate[:, t, :], hit[:, t, :], g1, None, ALU.mult)
                    else:
                        link(v.tensor_tensor(pick[:, t, :], pick[:, t, :], hit[:, t, :], ALU.add))
                        ins = v.scalar_tensor_tensor(gate[:, t, :], hit[:, t, :], g1, gate[:, t, :], ALU.mult, ALU.add)
                    if t == TT - 1 and j == TOPK - 1:
                        ins.then_inc(picks_ready, 1)
                    else:
                        link(ins)
            wait_full(dve, "rank")
            dve.wait_ge(picks_ready, 1)
            pos_v = tab4[:, :, 0:2].rearrange("p e a -> p a e")
            gate_v = tab4[:, :, 2:4].rearrange("p e a -> p a e")
            link(v.scalar_tensor_tensor(pos_v, bank_of("rank")[:, 0:2 * E].rearrange("p (a e) -> p a e", a=TT),
                                        ABSENT, pick, ALU.add, ALU.mult))
            free("rank", v.tensor_scalar(pos_v, pos_v, ABSENT, None, ALU.subtract))
            link(v.tensor_copy(gate_v, gate))
            wait_full(dve, "count")
            link(v.tensor_copy(count[0:E, :], bank_of("count")[0:E, 0:1]))
            link(v.tensor_scalar(rounds_c[0:E, :], count[0:E, :], float(CAP), 1.0, ALU.is_gt, ALU.add))
            for j in range(2, T // CAP):
                link(v.tensor_scalar(step[0:E, :], count[0:E, :], float(j * CAP), None, ALU.is_gt))
                link(v.tensor_tensor(rounds_c[0:E, :], rounds_c[0:E, :], step[0:E, :], ALU.add))
            free("count", v.tensor_copy(count[0:E, :], rounds_c[0:E, :]))
            wait_full(dve, "meta")
            link(v.tensor_scalar(meta_i[0:1, 0:E], bank_of("meta")[0:1, 0:E], 1.0, None, ALU.subtract))
            free("meta", v.tensor_copy(meta_i[0:1, E:2 * E], bank_of("meta")[0:1, E:2 * E]))
            wait_drained(dve, "meta")
            wait_full(dve, "gT")
            free("gT", v.tensor_copy(gT_sb[0:E, :], bank_of("gT")[0:E, 0:T]))
            for t in range(TT):
                for n in range(2):
                    job = f"bd{t}{n}"
                    wait_full(dve, job)
                    s = xs[:, t, n * BANK:(n + 1) * BANK]
                    free(job, v.tensor_tensor(s, bank_of(job)[:, :], s, ALU.add))
            wait_drained(dve, "bd11")
            dve.wait_ge(loaded["bup"], 32)

            def add_up(b):
                for t in range(TT):
                    for n in range(2):
                        dve.wait_ge(c_full, b * 4 + (2 * t + n + 1))
                        s = xs[:, t, n * BANK:(n + 1) * BANK]
                        v.tensor_tensor(s, banks[COMBINE[2 * t + n]][:, :], s, ALU.add).then_inc(y_added, 1)

            def onehot(b):
                dve.wait_ge(pt_full, b)
                dve.wait_ge(cols_ready, b + 1)
                for t in range(TT):
                    v.tensor_scalar(P2v[:, t, :], slot_row[:, :], cols[:, t:t + 1], None, ALU.is_equal).then_inc(p2_ready, 1)

            onehot(0)
            with dve.Fori(0, E) as e:
                extra = dve.value_load(meta_i[0:1, bass.ds(e, 1)], min_val=0, max_val=T // CAP - 1)
                first = dve.value_load(meta_i[0:1, bass.ds(e + E, 1)], min_val=0, max_val=E + T * TOPK // CAP)
                v.tensor_copy(bcol, bup_sb[:, bass.ds(e * (2 * KT), 2 * KT)]).then_inc(bcol_ready, 1)
                with dve.Fori(0, dve.snap(extra + 1)) as r:
                    b = dve.snap(first + r)
                    dve.wait_ge(up_steps, b * KT + KT)
                    v.tensor_copy(U_sb[:, :, 64:128].rearrange("p j q -> p q j"),
                                  banks[1][:, :].rearrange("p (q j) -> p q j", j=KT)).then_inc(u_by_v, 1)
                    add_up(b)
                    dve.wait_ge(bcol_ready, e + 1)
                    for i in range(2):
                        js = slice(4 * i, 4 * i + 4)
                        dve.wait_ge(t_full, b * 2 + (i + 1))
                        bias = bcol2[:, :, js].rearrange("p h j -> p j h").unsqueeze(3).broadcast_to([P, 4, 2, CAP])
                        v.tensor_tensor(A_sb[:, js], banks[2 + i][:, :].rearrange("p (j h t) -> p j h t", j=4, h=2),
                                        bias, ALU.add).then_inc(biased, 1)
                        dve.wait_ge(biased, b * 2 + (i + 1))
                        glu, lin = A_sb[:, js, 0, :], A_sb[:, js, 1, :]
                        v.tensor_scalar(glu, glu, LIMIT, None, ALU.min).then_inc(glu_ready, 1)
                        v.tensor_scalar(lin, lin, LIMIT, -LIMIT, ALU.min, ALU.max).then_inc(lin_ready, 1)
                        dve.wait_ge(glu_ready, b * 2 + (i + 1))
                        dve.wait_ge(lin_ready, b * 2 + (i + 1))
                        v.scalar_tensor_tensor(lin, lin, 1.0, glu, ALU.add, ALU.mult).then_inc(prod_ready, 1)
                        dve.wait_ge(prod_ready, b * 2 + (i + 1))
                        dve.wait_ge(sig_ready, b * 2 + (i + 1))
                        v.tensor_tensor(actT[:, js, :], lin, sig[:, js, :], ALU.mult).then_inc(act_ready, 1)
                    onehot(b + 1)
            last_b = dve.value_load(meta_i[0:1, 2 * E - 1:2 * E], min_val=0, max_val=E + T * TOPK // CAP)
            last_r = dve.value_load(meta_i[0:1, E - 1:E], min_val=0, max_val=T // CAP - 1)
            add_up(dve.snap(last_b + last_r + 1))
            rstd("out", 12, D)
            for t in range(TT):
                link(v.tensor_scalar(xs[:, t, :], xs[:, t, :], stat[:, 12 + t:13 + t], None, ALU.mult))
                v.tensor_tensor(xs[:, t, :], xs[:, t, :], gfin, ALU.mult).then_inc(fin_ready, 1)

        @block.tensor
        def _(pe):
            t_ = nc.tensor

            def begin(job):
                i = job_at[job]
                if i >= 8:
                    wait_drained(pe, JOBS[i - 8][0])
                return bank_of(job)

            def end(job, ins):
                ins.then_inc(full[full_at[job][0]], 1)

            def transposes(jobs, src):
                for i in range(4):
                    b = begin(f"{jobs}{i}")
                    for k in range(2):
                        for a in range(TT):
                            ins = t_.transpose(b[:, k * T + a * P:k * T + (a + 1) * P], src[:, a, 2 * i + k, :], ident[:, :])
                    end(f"{jobs}{i}", ins)

            pe.wait_ge(const_ready, N_CONST)
            pe.wait_ge(xn_ready, TT)
            pe.wait_ge(loaded["vrow1"], 16)
            pe.wait_ge(loaded["vrow2"], 80)
            b = begin("vec")
            t_.transpose(b[:, 0:TAPS * CT], vrow1[0:TAPS * CT, :], ident[0:TAPS * CT, 0:TAPS * CT])
            end("vec", t_.transpose(b[:, P:P + 15], vrow2[0:15, :], ident[0:15, 0:15]))
            transposes("hT", xn)
            wait_drained(pe, "hT3")
            for t in range(TT):
                b = begin(f"u{t}")
                for k in range(KT):
                    pe.wait_ge(loaded[f"win{k // 2}"], 16)
                    ins = t_.matmul(b[:, 0:TOK_COLS], hT[:, k, t * P:(t + 1) * P], w_in_sb[:, k, 0:TOK_COLS],
                                    start=k == 0, stop=k == KT - 1)
                end(f"u{t}", ins)
            pe.wait_ge(memn_ready, TT)
            transposes("mT", memn)
            for c in range(CT):
                b = begin(f"cv{c}")
                for g in range(2):
                    for k in range(KT):
                        at = TOK_COLS + g * CONV + c * P
                        ins = t_.matmul(b[:, g * T:(g + 1) * T], w_in_sb[:, k, at:at + P], hT[:, k, :],
                                        start=k == 0, stop=k == KT - 1)
                end(f"cv{c}", ins)
            pe.wait_ge(cq_ready, 4)
            b = begin("cqT")
            for k in range(2):
                for a in range(TT):
                    ins = t_.transpose(b[:, k * T + a * P:k * T + (a + 1) * P], u_tok[:, a, k * P:(k + 1) * P], ident[:, :])
            end("cqT", ins)
            b = begin("ckvT")
            for a in range(TT):
                ins = t_.transpose(b[:, a * P:(a + 1) * P], u_tok[:, a, Q_LORA:Q_LORA + KV_LORA], ident[:, :])
            end("ckvT", ins)
            b = begin("krT")
            pe.wait_ge(krow_ready, 1)
            for a in range(TT):
                ins = t_.transpose(b[0:QK, a * P:(a + 1) * P], krow[:, a, :], ident[:, :])
            end("krT", ins)
            wait_drained(pe, "cqT")
            pe.wait_ge(loaded["uq"], 16)
            for t in range(TT):
                for h in range(2):
                    b = begin(f"q{t}{h}")
                    for k in range(2):
                        ins = t_.matmul(b[:, 0:4 * QK], cqT[:, k, t * P:(t + 1) * P],
                                        uq_sb[:, k, h * 4 * QK:(h + 1) * 4 * QK], start=k == 0, stop=k == 1)
                    end(f"q{t}{h}", ins)
            wait_drained(pe, "ckvT")
            pe.wait_ge(loaded["ukv"], 16)
            for i in range(4):
                b = begin(f"kn{i}")
                for h in range(2):
                    ins = t_.matmul(b[0:NOPE, h * T:(h + 1) * T], ukv_sb[:, 2 * i + h, 0:NOPE], ckvT, start=True, stop=True)
                end(f"kn{i}", ins)
            for t in range(TT):
                b = begin(f"v{t}")
                end(f"v{t}", t_.matmul(b[:, :], ckvT[:, t * P:(t + 1) * P], ukv_sb[:, :, NOPE:], start=True, stop=True))

            def key_job(i):
                b = begin(f"xk{i}")
                for j in range(2):
                    for k in range(KT):
                        pe.wait_ge(loaded[f"wk{k // 4}"], 16)
                        at = (2 * i + j) * P
                        ins = t_.matmul(b[:, j * M:(j + 1) * M], wk_sb[:, k, at:at + P], mT[:, k, :],
                                        start=k == 0, stop=k == KT - 1)
                end(f"xk{i}", ins)

            def value_job(i):
                b = begin(f"xv{i}")
                a, n = divmod(i, 2)
                pe.wait_ge(loaded["wv"], 16)
                for k in range(KT):
                    ins = t_.matmul(b[:, :], mT[:, k, a * P:(a + 1) * P], wv_sb[:, k, n * BANK:(n + 1) * BANK],
                                    start=k == 0, stop=k == KT - 1)
                end(f"xv{i}", ins)

            wait_drained(pe, "mT3")
            key_job(0)
            key_job(1)
            pe.wait_ge(q_ready, TT)
            for i in range(4):
                b = begin(f"qT{i}")
                for h in range(2):
                    for a in range(TT):
                        ins = t_.transpose(b[0:QK, h * T + a * P:h * T + (a + 1) * P], q_tok[:, a, 2 * i + h, :], ident[:, :])
                end(f"qT{i}", ins)
            wait_drained(pe, "qT3")
            wait_drained(pe, "kn3")
            for i in range(2):
                b = begin(f"s0{i}")
                for h in range(4):
                    ins = t_.matmul(b[:, h * P:(h + 1) * P], qTs[0:QK, 4 * i + h, 0:P], KTs[0:QK, 4 * i + h, 0:P],
                                    start=True, stop=True)
                end(f"s0{i}", ins)
            for i in range(4):
                b = begin(f"s1{i}")
                for h in range(2):
                    ins = t_.matmul(b[:, h * T:(h + 1) * T], qTs[0:QK, 2 * i + h, P:T], KTs[0:QK, 2 * i + h, :],
                                    start=True, stop=True)
                end(f"s1{i}", ins)
            key_job(2)
            key_job(3)
            pe.wait_ge(e_ready, 1)
            for i in range(2):
                b = begin(f"pT0{i}")
                for h in range(4):
                    ins = t_.transpose(b[:, h * P:(h + 1) * P], S0[:, 4 * i + h, :], ident[:, :])
                end(f"pT0{i}", ins)
            pe.wait_ge(e_ready, 2)
            for i in range(4):
                b = begin(f"pT1{i}")
                for h in range(2):
                    for a in range(2):
                        ins = t_.transpose(b[:, (2 * h + a) * P:(2 * h + a + 1) * P],
                                           S1[:, 2 * i + h, a * P:(a + 1) * P], ident[:, :])
                end(f"pT1{i}", ins)
            wait_drained(pe, "pT13")
            for t in range(TT):
                b = begin(f"o{t}")
                for h in range(HEADS):
                    for a in range(t + 1):
                        lhs = PT0[:, h, :] if t == 0 else PT1[:, h, a, :]
                        ins = t_.matmul(b[:, h * VDIM:(h + 1) * VDIM], lhs, Vs[:, a, h * VDIM:(h + 1) * VDIM],
                                        start=a == 0, stop=a == t)
                end(f"o{t}", ins)
            value_job(0)
            value_job(1)
            wait_drained(pe, "o1")
            for t in range(TT):
                b = begin(f"oT{t}")
                for k in range(4):
                    ins = t_.transpose(b[:, k * P:(k + 1) * P], o_tok[:, t, k * P:(k + 1) * P], ident[:, :])
                end(f"oT{t}", ins)
            value_job(2)
            value_job(3)
            b = begin("mean")
            pe.wait_ge(conv_step, TAPS * CT)
            for c in range(CT):
                ins = t_.matmul(b[:, 0:T], mean_w[:, :], acc[:, c, :], start=c == 0, stop=c == CT - 1)
            end("mean", ins)
            b = begin("var")
            pe.wait_ge(zsq_ready, 1)
            for c in range(CT):
                ins = t_.matmul(b[:, 0:T], mean_w[:, :], sq4[:, c, :], start=c == 0, stop=c == CT - 1)
            end("var", ins)

            def project(jobs, src, w):
                for t in range(TT):
                    for n in range(2):
                        b = begin(f"{jobs}{t}{n}")
                        for k in range(KT):
                            ins = t_.matmul(b[:, :], src[:, k, t * P:(t + 1) * P], w[:, k, n * BANK:(n + 1) * BANK],
                                            start=k == 0, stop=k == KT - 1)
                        end(f"{jobs}{t}{n}", ins)

            wait_drained(pe, "oT1")
            pe.wait_ge(yconv_ready, 1)
            pe.wait_ge(loaded["wout"], 16)
            project("w", yT, wout_sb)
            pe.wait_ge(x1n_ready, TT)
            transposes("h2T", x1n)
            wait_drained(pe, "h2T3")
            pe.wait_ge(loaded["wxq"], 16)
            for i in range(4):
                b = begin(f"xq{i}")
                for j in range(2):
                    for k in range(KT):
                        at = (2 * i + j) * P
                        ins = t_.matmul(b[:, j * T:(j + 1) * T], wxq_sb[:, k, at:at + P], h2T[:, k, :],
                                        start=k == 0, stop=k == KT - 1)
                end(f"xq{i}", ins)
            wait_drained(pe, "xq3")
            for t in range(TT):
                for g in range(2):
                    b = begin(f"xs{t}{g}")
                    for h in range(2):
                        for k in range(2):
                            c = 2 * (2 * g + h) + k
                            ins = t_.matmul(b[:, h * M:(h + 1) * M], qT2[:, c, t * P:(t + 1) * P], kTm[:, c, :],
                                            start=k == 0, stop=k == 1)
                    end(f"xs{t}{g}", ins)
            for t in range(TT):
                pe.wait_ge(px_ready, t + 1)
                for g in range(2):
                    b = begin(f"xp{t}{g}")
                    for h in range(2):
                        for a in range(2):
                            ins = t_.transpose(b[:, (2 * h + a) * P:(2 * h + a + 1) * P],
                                               px[:, t, 2 * g + h, a * P:(a + 1) * P], ident[:, :])
                    end(f"xp{t}{g}", ins)
            wait_drained(pe, "xp11")
            for i in range(4):
                b = begin(f"xo{i}")
                for j in range(2):
                    for a in range(2):
                        c = 2 * i + j
                        ins = t_.matmul(b[:, j * T:(j + 1) * T], vm[:, a, c * P:(c + 1) * P], ptx[:, c // 2, a, :],
                                        start=a == 0, stop=a == 1)
                end(f"xo{i}", ins)
            wait_drained(pe, "xo3")
            pe.wait_ge(loaded["wxo"], 16)
            project("wo", oT2, wxo_sb)
            pe.wait_ge(rows_ready, TT)
            transposes("tT", rows)
            wait_drained(pe, "tT3")
            pe.wait_ge(loaded["router"], 32)
            b = begin("logits")
            for t in range(TT):
                for k in range(KT):
                    ins = t_.matmul(b[:, t * E:(t + 1) * E], tT[:, k, t * P:(t + 1) * P], wr3[:, k, :],
                                    start=k == 0, stop=k == KT - 1)
            end("logits", ins)
            pick = rt[:, 64:128].rearrange("p (a e) -> p a e", a=TT)
            gate = rt[:, 128:192].rearrange("p (a e) -> p a e", a=TT)
            b = begin("rank")
            pe.wait_ge(picks_ready, 1)
            t_.matmul(b[:, 0:E], before[:, :], pick[:, 0, :], start=True, stop=True)
            t_.matmul(b[:, E:2 * E], ones[:, :], pick[:, 0, :], start=True, stop=False)
            end("rank", t_.matmul(b[:, E:2 * E], before[:, :], pick[:, 1, :], start=False, stop=True))
            b = begin("count")
            t_.matmul(b[0:E, 0:1], pick[:, 0, :], ones[:, 0:1], start=True, stop=False)
            end("count", t_.matmul(b[0:E, 0:1], pick[:, 1, :], ones[:, 0:1], start=False, stop=True))
            b = begin("meta")
            wait_drained(pe, "count")
            end("meta", t_.matmul(b[0:1, 0:2 * E], rt[0:E, 308:309], sel32[0:E, :], start=True, stop=True))
            b = begin("gT")
            t_.transpose(b[0:E, 0:P], gate[:, 0, :], ident[:, :])
            end("gT", t_.transpose(b[0:E, P:T], gate[:, 1, :], ident[:, :]))
            wait_drained(pe, "gT")
            pe.wait_ge(loaded["late"], 32)
            for t in range(TT):
                for n in range(2):
                    b = begin(f"bd{t}{n}")
                    end(f"bd{t}{n}", t_.matmul(b[:, :], rt[0:E, 320 + t * P:320 + (t + 1) * P],
                                               bdown_sb[0:E, n * BANK:(n + 1) * BANK], start=True, stop=True))

            wait_drained(pe, "bd11")
            pe.wait_ge(zeroed, 2)

            def gather(b):
                pe.wait_ge(p2_ready, b * 2 + 2)
                for a in range(TT):
                    for h in range(2):
                        ins = t_.matmul(banks[4][h * 64:(h + 1) * 64, :], P2v[:, a, h * 64:(h + 1) * 64],
                                        rows[:, a, 4 * h:4 * h + 4, :], start=a == 0, stop=a == 1)
                ins.then_inc(g_full, 1)

            def gather_columns(b):
                pe.wait_ge(g_copied, b + 1)
                for c in range(4):
                    ins = t_.transpose(banks[2][:, c * P:(c + 1) * P], G_sb[:, c * P:(c + 1) * P], ident[:, :])
                ins.then_inc(x_full, 1)

            def combine():
                for a in range(TT):
                    for h in range(2):
                        t_.matmul(banks[COMBINE[2 * a + h]][:, :], PT2[h * 64:(h + 1) * 64, a * P:(a + 1) * P],
                                  y_sb[h * 64:(h + 1) * 64, :], start=True, stop=True).then_inc(c_full, 1)

            gather(0)
            gather_columns(0)
            with pe.Fori(0, E // 2) as pair:
                for odd in range(2):
                    e = pair * 2 + odd
                    up0 = 0 if odd else 8
                    extra = pe.value_load(meta_i[0:1, bass.ds(e, 1)], min_val=0, max_val=T // CAP - 1)
                    first = pe.value_load(meta_i[0:1, bass.ds(e + E, 1)], min_val=0, max_val=E + T * TOPK // CAP)
                    with pe.Fori(0, pe.snap(extra + 1)) as r:
                        n = pe.snap(first + r)
                        pe.wait_ge(xg_ready, n + 1)
                        for k in range(KT):
                            pe.wait_ge(slab_in[up0 + k], pair * 16 + 16)
                            w = slab(up0 + k)
                            for c in range(2):
                                for h in range(2):
                                    ins = t_.matmul(banks[c][h * 64:(h + 1) * 64, :], xg[:, k, :],
                                                    w[:, h * FF + c * BANK:h * FF + (c + 1) * BANK],
                                                    start=k == 0, stop=k == KT - 1)
                            ins.then_inc(up_steps, 1)
                        pe.wait_ge(y_ready, n)
                        pe.wait_ge(pt_copied, n)
                        pe.wait_ge(y_added, n * 4)
                        combine()
                        pe.wait_ge(u_by_a, n + 1)
                        pe.wait_ge(u_by_v, n + 1)
                        for j in range(KT):
                            ins = t_.transpose(banks[2 + j // 4][:, (j % 4) * P:(j % 4 + 1) * P], U_sb[:, j, :], ident[:, :])
                            if j % 4 == 3:
                                ins.then_inc(t_full, 1)
                        pe.wait_ge(y_added, n * 4 + 1)
                        for a in range(TT):
                            t_.transpose(banks[6][:, a * P:(a + 1) * P], P2v[:, a, :], ident[:, :])
                        for a in range(TT):
                            ins = t_.matmul(banks[6][:, T:T + 1], P2v[:, a, :], cols[:, 2 + a:3 + a], start=a == 0, stop=a == 1)
                        ins.then_inc(pt_full, 1)
                        pe.wait_ge(y_added, n * 4 + 4)
                        for j in range(KT):
                            if j == 2:
                                gather(n + 1)
                            if j == 6:
                                gather_columns(n + 1)
                            pe.wait_ge(act_ready, n * 2 + (j // 4 + 1))
                            if j % 2 == 0:
                                pe.wait_ge(slab_in[16 + j // 2], e * 16 + 16)
                            w = slab(16 + j // 2)[:, (j % 2) * D:(j % 2 + 1) * D]
                            for h in range(2):
                                ins = t_.matmul(banks[5][h * 64:(h + 1) * 64, :], actT[:, j, :], w[:, h * BANK:(h + 1) * BANK],
                                                start=j == 0, stop=j == KT - 1)
                            if j % 2 == 1:
                                ins.then_inc(down_steps, 1)
            last_b = pe.value_load(meta_i[0:1, 2 * E - 1:2 * E], min_val=0, max_val=E + T * TOPK // CAP)
            last_r = pe.value_load(meta_i[0:1, E - 1:E], min_val=0, max_val=T // CAP - 1)
            blocks = pe.snap(last_b + last_r + 1)
            pe.wait_ge(y_ready, blocks)
            pe.wait_ge(y_added, blocks * 4)
            combine()


_INS = ['x', 'mem', 'positions', 'g_mix', 'w_in', 'g_q', 'w_uq', 'g_kv', 'w_ukv', 'w_dw', 'b_dw', 'g_conv_ln',
        'b_conv_ln', 'w_out', 'g_xattn', 'g_mem', 'w_xq', 'w_xkv', 'w_xo', 'g_ffn', 'w_router', 'b_router',
        'w_up', 'b_up', 'w_down', 'b_down', 'g_final']


def kernel(**inputs):
    import concourse.bacc as bacc
    from concourse.bass_utils import run_bass_kernel_spmd

    nc = bacc.Bacc("TRN2", target_bir_lowering=False, num_devices=1)
    arrays, args = {}, []
    for name in _INS:
        a = np.ascontiguousarray(inputs[name])
        arrays[f"in_{name}_dram"] = a
        args.append(nc.dram_tensor(f"in_{name}_dram", a.shape, mybir.dt.from_np(a.dtype), kind="ExternalInput").ap())
    args.append(nc.dram_tensor("out_dram", (1, T, D), mybir.dt.float32, kind="ExternalOutput").ap())
    build_program(nc, *args)
    r = run_bass_kernel_spmd(nc, [arrays], core_ids=[0])
    return r.results[0]["out_dram"]
```

```python
import numpy as np
import concourse.bass as bass
from concourse import mybir
from contextlib import ExitStack

D = 1024
T = 256
M = 256
P = 128
KT = D // P
TT = T // P
CHUNK = 64
HEADS, NOPE, ROPE, VDIM = 8, 64, 32, 64
QK = NOPE + ROPE
Q_LORA, KV_LORA = 256, 128
CONV, TAPS = 512, 31
CT = CONV // P
CONV_V = 3
TOK_COLS = Q_LORA + KV_LORA + ROPE
IN_COLS = TOK_COLS + 2 * CONV
XH, XD = 4, 256
E, TOPK, FF = 32, 4, 1024
CAP = 64
LIMIT, ALPHA = 7.0, 1.702
EPS = 1e-5
ROPE_THETA = 10000.0
MASKED = -1e30
TURN = E // 4 + 1
ABSENT = 4096.0
SLAB = 2 * D
NVEC = 15 + 4 * KT
BANK = 512


def trunk_jobs():
    jobs = [("vec", "v", "v")]
    jobs += [(f"hT{i}", "v", "v") for i in range(4)]
    jobs += [(f"u{t}", "v", "v") for t in range(2)]
    jobs += [(f"cv{c}", "a", "v") for c in range(4)]
    jobs += [(f"mT{i}", "a", "a") for i in range(4)]
    jobs += [(f"xk{i}", "a", "a") for i in range(2)]
    jobs += [("cqT", "v", "v"), ("ckvT", "v", "v"), ("krT", "a", "a")]
    jobs += [(f"q{t}{h}", "a", "a") for t in range(2) for h in range(2)]
    jobs += [(f"kn{i}", "a", "a") for i in range(4)]
    jobs += [(f"v{t}", "a", "a") for t in range(2)]
    jobs += [(f"qT{i}", "a", "a") for i in range(4)]
    jobs += [(f"s0{i}", "v", "v") for i in range(2)]
    jobs += [(f"s1{i}", "v", "v") for i in range(4)]
    jobs += [(f"xk{i}", "a", "a") for i in range(2, 4)]
    jobs += [(f"pT0{i}", "a", "a") for i in range(2)]
    jobs += [(f"pT1{i}", "a", "a") for i in range(4)]
    jobs += [(f"o{t}", "v", "v") for t in range(2)]
    jobs += [("xv0", "a", "a")]
    jobs += [(f"oT{t}", "v", "v") for t in range(2)]
    jobs += [("mean", "v", "v"), ("var", "a", "v"), ("xv1", "a", "a"), ("xv2", "a", "a")]
    jobs += [(f"w{t}{n}", "v", "v") for t in range(2) for n in range(2)]
    jobs += [("h2T00", "v", "v"), ("h2T01", "v", "v"), ("h2T10", "v", "v"), ("h2T11", "v", "v")]
    jobs += [(f"xq{i}", "a", "a") for i in range(4)]
    jobs += [(f"xs{t}{g}", "v", "v") for t in range(2) for g in range(2)]
    jobs += [("xv3", "a", "a")]
    jobs += [(f"xp{t}{g}", "a", "a") for t in range(2) for g in range(2)]
    jobs += [(f"xo{i}", "a", "a") for i in range(4)]
    jobs += [(f"wo{t}{n}", "v", "v") for t in range(2) for n in range(2)]
    jobs += [(f"tT{t}{i}", "v", "v") for t in range(2) for i in range(2)]
    jobs += [("lg0", "v", "v"), ("lg1", "v", "v")]
    jobs += [("count", "v", "v"), ("rank", "v", "v"), ("meta", "v", "v"), ("gT", "a", "a")]
    return jobs


def build_program(nc, x, mem, positions, g_mix, w_in, g_q, w_uq, g_kv, w_ukv, w_dw, b_dw, g_conv_ln,
                  b_conv_ln, w_out, g_xattn, g_mem, w_xq, w_xkv, w_xo, g_ffn, w_router, b_router,
                  w_up, b_up, w_down, b_down, g_final, out):
    fp32, i32, u32 = mybir.dt.float32, mybir.dt.int32, mybir.dt.uint32
    ALU = mybir.AluOpType
    ACT = mybir.ActivationFunctionType
    AX = mybir.AxisListType

    ctx = ExitStack()
    with ctx:
        def sb(name, cols, dt=fp32):
            return ctx.enter_context(nc.sbuf_tensor(name, [P, cols], dt))

        def sem(name):
            return ctx.enter_context(nc.semaphore(name))

        ring = sb("ring", 20 * SLAB)

        def slab(i, n=1):
            return ring[:, i * SLAB:(i + n) * SLAB]

        def carve(base, sizes):
            found = {}
            for name, n in sizes:
                found[name] = (base, n)
                base += n
            return found, base

        w_in_sb = ring[:, 0:KT * IN_COLS].rearrange("p (k n) -> p k n", k=KT)
        low, end = carve(KT * IN_COLS, [
            ("uq", 2 * HEADS * QK), ("ukv", HEADS * (NOPE + VDIM)), ("cqT", 2 * T), ("ckvT", T),
            ("krow", TT * QK), ("mask", TT * T), ("vrow1", P), ("vrow2", P), ("sg", 2 * T), ("trig", 2 * TT * 16)])
        assert end <= 8 * SLAB
        high, end = carve(8 * SLAB, [
            ("u", TT * TOK_COLS), ("qtok", TT * HEADS * QK), ("KT", HEADS * T), ("qT", HEADS * T),
            ("V", TT * HEADS * VDIM), ("S0", HEADS * P), ("S1", HEADS * T), ("PT0", HEADS * P),
            ("PT1", HEADS * T), ("z", CT * (TAPS - 1 + T)), ("acc", CT * T),
            ("freq", 16), ("pos", 2 * TT)])
        assert end <= 16 * SLAB

        def part(name):
            base, n = low[name] if name in low else high[name]
            return ring[:, base:base + n]

        uq_sb = part("uq").rearrange("p (k n) -> p k n", k=2)
        ukv_sb = part("ukv").rearrange("p (h n) -> p h n", h=HEADS)
        cqT = part("cqT").rearrange("p (k t) -> p k t", k=2)
        ckvT = part("ckvT")
        krow = part("krow").rearrange("p (a n) -> p a n", a=TT)
        mask = part("mask").rearrange("p (a k) -> p a k", a=TT)
        vrow1, vrow2 = part("vrow1"), part("vrow2")
        sg = part("sg").rearrange("p (a t) -> p a t", a=2)
        trig = part("trig").rearrange("p (f a j) -> p f a j", f=2, a=TT)
        u_tok = part("u").rearrange("p (a n) -> p a n", a=TT)
        q_tok = part("qtok").rearrange("p (a h n) -> p a h n", a=TT, h=HEADS)
        KTs = part("KT").rearrange("p (h t) -> p h t", h=HEADS)
        qTs = part("qT").rearrange("p (h t) -> p h t", h=HEADS)
        Vs = part("V").rearrange("p (a n) -> p a n", a=TT)
        S0 = part("S0").rearrange("p (h k) -> p h k", h=HEADS)
        S1 = part("S1").rearrange("p (h k) -> p h k", h=HEADS)
        PT0 = part("PT0").rearrange("p (h q) -> p h q", h=HEADS)
        PT1 = part("PT1").rearrange("p (h a q) -> p h a q", h=HEADS, a=TT)
        z = part("z").rearrange("p (c t) -> p c t", c=CT)
        acc = part("acc").rearrange("p (c t) -> p c t", c=CT)
        o_tok = part("S0").rearrange("p (a n) -> p a n", a=TT)
        rtmp = part("S1")[:, 0:4 * HEADS * 16].rearrange("p (i h j) -> p i h j", i=4, h=HEADS)
        ktmp = part("S1")[:, 512:512 + 4 * TT * 16].rearrange("p (i a j) -> p i a j", i=4, a=TT)
        ttmp = part("S0")[:, 0:8 * TT * 16].rearrange("p (i a j) -> p i a j", i=8, a=TT)
        sq4 = part("qtok")[:, 0:CT * T].rearrange("p (c t) -> p c t", c=CT)
        rstd_t = part("u")[:, 0:T]
        qT2 = slab(12).rearrange("p (k t) -> p k t", k=KT)
        px = slab(13).rearrange("p (a h m) -> p a h m", a=TT, h=XH)
        ptx = slab(14).rearrange("p (h a q) -> p h a q", h=XH, a=M // P)
        wk_sb = slab(16, 4).rearrange("p (k n) -> p k n", k=KT)
        wout_sb = slab(16, 4).rearrange("p (k n) -> p k n", k=KT)
        wv_sb = slab(0, 4).rearrange("p (k n) -> p k n", k=KT)
        wxq_sb = slab(4, 4).rearrange("p (k n) -> p k n", k=KT)
        wxo_sb = slab(16, 4).rearrange("p (k n) -> p k n", k=KT)

        buf_x = sb("buf_x", TT * D)
        buf_f = sb("buf_f", KT * T)
        buf_m = sb("buf_m", KT * T)
        buf_k = sb("buf_k", KT * T)
        buf_v = sb("buf_v", TT * D)
        xs = buf_x[:, :].rearrange("p (a n) -> p a n", a=TT)
        hT = buf_f[:, :].rearrange("p (k t) -> p k t", k=KT)
        yT = hT
        conv_prod = buf_f[:, D:2 * D].rearrange("p (i t) -> p i t", i=4)
        h2T = hT
        tT = hT
        mT = buf_m[:, :].rearrange("p (k t) -> p k t", k=KT)
        oT2 = mT
        mem_sb = buf_k[:, :].rearrange("p (a n) -> p a n", a=TT)
        kTm = buf_k[:, :].rearrange("p (k m) -> p k m", k=KT)
        rows = buf_k[:, :].rearrange("p (a k q) -> p a k q", a=TT, k=KT)
        xn = buf_v[:, :].rearrange("p (a k q) -> p a k q", a=TT, k=KT)
        vm = buf_v[:, :].rearrange("p (a n) -> p a n", a=TT)
        gfin = buf_v[:, 0:D]
        gffn = gfin
        memn = part("PT1").rearrange("p (a k q) -> p a k q", a=TT, k=KT)

        ident = sb("ident", P)
        ones = sb("ones", P)
        mean_w = sb("mean_w", P)
        before = sb("before", P)
        slot_row = sb("slot_row", P)
        e_row = sb("e_row", E)
        sel32 = sb("sel32", 2 * E)
        wr_sb = sb("wr_sb", KT * E)
        br_sb = sb("br_sb", E)
        bup_sb = sb("bup_sb", E * 2 * KT)
        taps = sb("taps", TAPS * CT)
        vecs = sb("vecs", NVEC)
        gmix_sb, gm_sb, gx_sb, gf_sb = (vecs[:, 15 + i * KT:15 + (i + 1) * KT] for i in range(4))
        stat = sb("stat", 48)
        roots = sb("roots", 14)
        newton = sb("newton", 2)
        scrap = sb("scrap", 4)
        eps = sb("eps", 1)
        freq = part("freq")
        pos_i = part("pos")[:, 0:TT].bitcast(i32)
        pos_f = part("pos")[:, TT:2 * TT]
        table = sb("table", E * 4)
        meta_i = sb("meta_i", 2 * E, i32)
        cols = buf_v[:, D + 260:D + 264]
        gates2 = buf_v[:, D + 288:D + 288 + TT * P].rearrange("p (a s) -> p a s", a=TT)
        passed = buf_v[:, D + 800:D + 804]
        cap_row = buf_v[:, D + 804:D + 808]
        bcol = buf_v[:, D + 264:D + 280]
        P2 = buf_v[:, D:D + TT * P]
        PT2 = wr_sb
        gslot = buf_v[:, D + 256:D + 257]
        G_sb = buf_v[:, D + 288:D + 800]
        wr3 = wr_sb[:, :].rearrange("p (k e) -> p k e", k=KT)
        tab4 = table[:, :].rearrange("p (e c) -> p e c", c=4)
        bup4 = bup_sb[:, :].rearrange("p (e h j) -> p e h j", e=E, h=2)
        bcol2 = bcol.rearrange("p (h j) -> p h j", h=2)
        P2v = P2.rearrange("p (a s) -> p a s", a=TT)
        U_sb = buf_f[:, 0:1024].rearrange("p (j q) -> p j q", j=KT)
        A_sb = buf_f[:, 1024:2048].rearrange("p (j h t) -> p j h t", j=KT, h=2)
        xg = buf_m[:, 0:512].rearrange("p (k s) -> p k s", k=KT)
        sig = buf_m[:, 512:1024].rearrange("p (j t) -> p j t", j=KT)
        actT = buf_m[:, 1024:1536].rearrange("p (j t) -> p j t", j=KT)
        y_sb = buf_m[:, 1536:2048]
        COMBINE = (6, 7, 4, 5)
        rt = buf_m

        banks = [ctx.enter_context(nc.psum_tensor(f"bank{i}", [P, BANK], fp32)) for i in range(8)]

        full = {"v": sem("psum_full_for_vector"), "a": sem("psum_full_for_scalar")}
        drained = {"v": sem("psum_drained_by_vector"), "a": sem("psum_drained_by_scalar")}
        JOBS = trunk_jobs()
        job_at = {name: i for i, (name, _, _) in enumerate(JOBS)}
        full_at, drained_at = {}, {}
        for name, first, last in JOBS:
            full_at[name] = (first, 1 + sum(1 for n, f, _ in JOBS[:job_at[name]] if f == first))
            drained_at[name] = (last, 1 + sum(1 for n, _, l in JOBS[:job_at[name]] if l == last))
        NDRAIN = {s: sum(1 for j in JOBS if j[2] == s) for s in "va"}

        def bank_of(job):
            return banks[job_at[job] % 8]

        def wait_full(eng, job):
            eng.wait_ge(full[full_at[job][0]], full_at[job][1])

        def wait_drained(eng, job):
            eng.wait_ge(drained[drained_at[job][0]], drained_at[job][1])

        names = ["x0", "x1", "mem", "pos", "vrow1", "vrow2", "win0", "win1", "win2", "win3", "uq", "ukv", "wk0",
                 "wk1", "wv", "wout", "wxq0", "wxq1", "wxo", "bdown", "router", "bup", "gffn", "late"]
        loaded = {n: sem(f"loaded_{n}") for n in names}
        const_ready = sem("const_ready")
        v_chain = sem("vector_step")
        conv_step = sem("conv_step")
        conv_pool_step = sem("conv_pool_step")
        conv_prod_ready = sem("conv_product_ready")
        a_chain = sem("scalar_step")
        x_squares = sem("x_squares_summed")
        m_squares = sem("mem_squares_summed")
        xn_ready = sem("normed_x_ready")
        memn_ready = sem("normed_mem_ready")
        root_ready = sem("root_mean_square_ready")
        ROOTS = ["x", "mem", "cq", "ckv", "var", "x1", "x2", "out0", "out1"]

        def wait_root(eng, name):
            eng.wait_ge(root_ready, 1 + ROOTS.index(name))

        trig_arg = sem("angles_ready")
        trig_ready = sem("cos_sin_ready")
        cq_squares = sem("latent_squares_summed")
        cq_ready = sem("normed_latents_ready")
        krow_ready = sem("rotated_key_ready")
        gate_sig = sem("conv_gate_sigmoid_ready")
        q_ready = sem("rotated_q_ready")
        s_ready = sem("mla_scores_ready")
        e_ready = sem("mla_exp_ready")
        zsq_ready = sem("conv_squares_ready")
        ln_ready = sem("conv_layernorm_ready")
        lnsig_ready = sem("conv_swish_sigmoid_ready")
        yconv_ready = sem("conv_output_ready")
        x1_squares = sem("x1_squares_summed")
        x1_scale = sem("x1_scale_ready")
        xe_ready = sem("cross_exp_ready")
        px_ready = sem("cross_probs_ready")
        x2_squares = sem("x2_squares_summed")
        x2_scale = sem("x2_scale_ready")
        rows_normed = sem("rows_normed")
        rows_ready = sem("expert_rows_ready")
        top_ready = sem("top_values_ready")
        topexp_ready = sem("top_exp_ready")
        picks_ready = sem("picks_ready")
        gates_ready = sem("gates_ready")
        table_ready = sem("ranks_and_gates_in_table")
        slab_in = [sem(f"slab{i}_in") for i in range(20)]
        p2_ready = sem("onehot_ready")
        pt_full = sem("transposed_onehot_full")
        pt_copied = sem("transposed_onehot_copied")
        g_full = sem("gathered_rows_full")
        g_copied = sem("gathered_rows_copied")
        x_full = sem("gathered_columns_full")
        xg_ready = sem("gathered_columns_ready")
        up_steps = sem("up_slabs_used")
        u_by_a = sem("up_drained_by_scalar")
        u_by_v = sem("up_drained_by_vector")
        t_full = sem("up_transposed_full")
        biased = sem("up_biased")
        glu_ready = sem("glu_ready")
        lin_ready = sem("lin_ready")
        prod_ready = sem("glu_lin_ready")
        sig_ready = sem("glu_sigmoid_ready")
        act_ready = sem("act_ready")
        down_steps = sem("down_slabs_used")
        y_ready = sem("y_scaled_ready")
        c_full = sem("combined_full")
        y_added = sem("y_added")
        cols_ready = sem("expert_columns_ready")
        passed_ready = sem("passed_ranks_ready")
        bcol_ready = sem("expert_bias_ready")
        cap_set = sem("pool_constants_set")
        zeroed = sem("first_combine_zeroed")
        fin_squares = sem("final_squares_summed")
        fin_ready = sem("output_ready")
        stored = sem("output_stored")

        block = ctx.enter_context(nc.Block())

        kp = "(k p) n -> p k n"
        up_v = w_up[0].rearrange("e (k p) n -> e p k n", p=P)
        down_v = w_down[0].rearrange("e (p k) n -> e p (k n)", k=KT)

        def krowsq(i):
            return part("PT0")[:, i * T:(i + 1) * T]

        @block.sync
        def _(sp):
            for t in range(TT):
                sp.dma_start(xs[:, t, :], x[0, t * P:(t + 1) * P, :]).then_inc(loaded[f"x{t}"], 16)
            sp.dma_start(vrow1[0:TAPS * CT, :], w_dw[0].rearrange("w (c p) -> (w c) p", p=P)).then_inc(loaded["vrow1"], 16)
            at = 0
            for vec, n in ((b_dw, CT), (g_conv_ln, CT), (b_conv_ln, CT), (g_q, 2), (g_kv, 1), (g_mix, KT), (g_mem, KT),
                           (g_xattn, KT), (g_ffn, KT)):
                sp.dma_start(vrow2[at:at + n, :], vec[0].rearrange("(c p) -> c p", p=P)).then_inc(loaded["vrow2"], 16)
                at += n
            sp.dma_start(pos_i, positions[0].rearrange("(a p) -> p a", p=P), allow_slow_non_contiguous=True).then_inc(loaded["pos"], 16)
            w_in_v = w_in[0].rearrange(kp, p=P)
            for i in range(4):
                sp.dma_start(w_in_sb[:, 2 * i:2 * i + 2, :], w_in_v[:, 2 * i:2 * i + 2, :]).then_inc(loaded[f"win{i}"], 16)
            sp.dma_start(mem_sb, mem[0].rearrange("(a p) n -> p a n", p=P)).then_inc(loaded["mem"], 16)
            w_xkv_v = w_xkv[0].rearrange(kp, p=P)
            for i in range(2):
                sp.dma_start(wk_sb[:, 4 * i:4 * i + 4, :], w_xkv_v[:, 4 * i:4 * i + 4, 0:D]).then_inc(loaded[f"wk{i}"], 16)
            sp.dma_start(uq_sb, w_uq[0].rearrange(kp, p=P)).then_inc(loaded["uq"], 16)
            sp.dma_start(ukv_sb, w_ukv[0].rearrange("p (h n) -> p h n", h=HEADS)).then_inc(loaded["ukv"], 16)
            sp.dma_start(wr3, w_router[0].rearrange(kp, p=P)).then_inc(loaded["router"], 16)
            sp.dma_start(br_sb[:, :], b_router[0:1, :].broadcast_to([P, E])).then_inc(loaded["router"], 16)
            wait_drained(sp, "cv3")
            sp.dma_start(wv_sb, w_xkv_v[:, :, D:2 * D]).then_inc(loaded["wv"], 16)
            bup_v = b_up[0].rearrange("e (h p j) -> p e h j", h=2, j=KT)
            for h in range(2):
                sp.dma_start(bup4[:, :, h, :], bup_v[:, :, h, :]).then_inc(loaded["bup"], 16)
            wait_drained(sp, "xk3")
            sp.dma_start(wout_sb, w_out[0].rearrange(kp, p=P)).then_inc(loaded["wout"], 16)
            wait_drained(sp, "s13")
            w_xq_v = w_xq[0].rearrange(kp, p=P)
            for i in range(2):
                sp.dma_start(wxq_sb[:, 4 * i:4 * i + 4, :], w_xq_v[:, 4 * i:4 * i + 4, :]).then_inc(loaded[f"wxq{i}"], 16)

            def load_up(e, base, ks):
                for k in ks:
                    sp.dma_start(slab(base + k), up_v[e, :, k, :]).then_inc(slab_in[base + k], 16)

            def load_down(e):
                for s in range(4):
                    sp.dma_start(slab(16 + s), down_v[e, :, s * SLAB:(s + 1) * SLAB]).then_inc(slab_in[16 + s], 16)

            wait_drained(sp, "oT1")
            sp.wait_ge(yconv_ready, 1)
            load_up(0, 8, (0, 1, 2, 3, 7))
            wait_drained(sp, "w11")
            sp.dma_start(wxo_sb, w_xo[0].rearrange(kp, p=P)).then_inc(loaded["wxo"], 16)
            wait_drained(sp, "xq3")
            load_up(1, 0, range(4, 8))
            wait_drained(sp, "xs11")
            load_up(0, 8, [4])
            wait_drained(sp, "xv3")
            load_up(1, 0, range(0, 4))
            wait_drained(sp, "xo3")
            sp.dma_start(gffn, g_ffn[0:1, :].broadcast_to([P, D])).then_inc(loaded["gffn"], 16)
            load_up(0, 8, (5, 6))
            wait_drained(sp, "wo11")
            sp.wait_ge(zeroed, 1)
            for h in range(2):
                sp.dma_start(y_sb[h * 64:h * 64 + E, :], b_down[0, :, h * BANK:(h + 1) * BANK]).then_inc(loaded["bdown"], 16)
            load_down(0)
            sp.wait_ge(rows_ready, TT)
            sp.dma_start(gfin, g_final.rearrange("(a n) -> a n", a=1).broadcast_to([P, D])).then_inc(loaded["late"], 16)

            wait_drained(sp, "meta")

            def last_block(e):
                extra = sp.value_load(meta_i[0:1, bass.ds(e, 1)], min_val=0, max_val=T // CAP - 1)
                first = sp.value_load(meta_i[0:1, bass.ds(e + E, 1)], min_val=0, max_val=E + T * TOPK // CAP)
                return sp.snap(first + extra)

            def replace_up(e, n, base):
                for k in range(KT):
                    sp.wait_ge(up_steps, n * KT + (k + 1))
                    load_up(e, base, [k])

            def replace_down(e, n):
                for s in range(4):
                    sp.wait_ge(down_steps, n * 4 + (s + 1))
                    sp.dma_start(slab(16 + s), down_v[e, :, s * SLAB:(s + 1) * SLAB]).then_inc(slab_in[16 + s], 16)

            with sp.Fori(0, TURN) as pair:
                e = pair * 2
                n = last_block(e)
                replace_up(e + 2, n, 8)
                replace_down(e + 1, n)
                n = last_block(e + 1)
                replace_up(e + 3, n, 0)
                replace_down(e + 2, n)
            replace_down(2 * TURN + 1, last_block(2 * TURN))
            with sp.Fori(TURN + 1, E // 2) as pair:
                e = pair * 2
                n = last_block(e - 1)
                replace_up(e, last_block(e - 2), 8)
                replace_down(e, n)
                replace_up(e + 1, n, 0)
                replace_down(e + 1, last_block(e))
            for a in range(TT):
                sp.wait_ge(fin_ready, a + 1)
                sp.dma_start(out[0, a * P:(a + 1) * P, :], xs[:, a, :]).then_inc(stored, 16)
            sp.wait_ge(stored, 16 * TT)

        @block.gpsimd
        def _(pool):
            g = nc.gpsimd
            steps = [0]

            def done(ins):
                steps[0] += 1
                ins.then_inc(const_ready, 1)
                pool.wait_ge(const_ready, steps[0])

            done(g.memset(eps[:, :], EPS))
            done(g.memset(ident[:, :], 0.0))
            done(g.affine_select(out=ident[:, :], in_=ident[:, :], compare_op=ALU.not_equal, fill=1.0,
                                 base=0, pattern=[[-1, P]], channel_multiplier=1))
            for j in range(16):
                done(g.memset(freq[:, j:j + 1], float(np.float32(ROPE_THETA) ** np.float32(-2.0 * j / ROPE))))
            done(g.memset(ones[:, :], 1.0))
            done(g.memset(mean_w[:, :], 1.0 / CONV))
            done(g.affine_select(out=before[:, :], in_=ones[:, :], compare_op=ALU.is_gt, fill=0.0,
                                 base=0, pattern=[[1, P]], channel_multiplier=-1))
            done(g.affine_select(out=sel32[0:E, E:2 * E], in_=ones[0:E, 0:E], compare_op=ALU.is_gt, fill=0.0,
                                 base=0, pattern=[[1, E]], channel_multiplier=-1))
            done(g.tensor_copy(sel32[0:E, 0:E], ident[0:E, 0:E]))
            done(g.iota(slot_row[:, :], pattern=[[0, 2], [1, CAP]], base=0, channel_multiplier=0,
                        allow_small_or_imprecise_dtypes=True))
            done(g.iota(e_row[:, :], pattern=[[1, E]], base=0, channel_multiplier=0,
                        allow_small_or_imprecise_dtypes=True))
            done(g.memset(mask, 0.0))
            for a in range(TT):
                for c in range(P // CHUNK):
                    seen = a * P + (c + 1) * CHUNK
                    if seen < T:
                        done(g.memset(mask[c * CHUNK:(c + 1) * CHUNK, a, seen:T], MASKED))
            done(g.memset(krow, 0.0))
            done(g.memset(z[:, :, 0:TAPS - 1], 0.0))

            wait_drained(pool, "vec")
            wait_drained(pool, f"cv{CT - 1}")
            n = 0
            for w in range(TAPS):
                for c in range(CONV_V, CT):
                    src, wt = z[:, c, w:w + T], taps[:, w * CT + c:w * CT + c + 1]
                    prod = conv_prod[:, n % 4, :]
                    if w == 0:
                        g.tensor_scalar(acc[:, c, :], src, wt, vecs[:, c:c + 1], ALU.mult, ALU.add).then_inc(conv_pool_step, 1)
                    else:
                        g.tensor_scalar(prod, src, wt, None, ALU.mult).then_inc(conv_prod_ready, 1)
                        pool.wait_ge(conv_prod_ready, n - (CT - CONV_V) + 1)
                        pool.wait_ge(conv_pool_step, n - (CT - CONV_V) + 1)
                        g.tensor_tensor(acc[:, c, :], acc[:, c, :], prod, ALU.add).then_inc(conv_pool_step, 1)
                    n += 1

            wait_drained(pool, "xo3")
            g.memset(cap_row[:, 0:TT], float(CAP)).then_inc(cap_set, 1)
            g.memset(cap_row[:, TT:], 0.0).then_inc(cap_set, 1)
            g.memset(gates2, 0.0).then_inc(cap_set, 1)
            pool.wait_ge(cap_set, 3)
            pool.wait_ge(loaded["gffn"], 16)
            for t in range(TT):
                pool.wait_ge(rows_normed, t + 1)
                r = rows[:, t].rearrange("p k q -> p (k q)")
                g.tensor_tensor(r, r, gffn, ALU.mult).then_inc(rows_ready, 1)
            wait_drained(pool, "wo11")
            g.memset(y_sb, 0.0).then_inc(zeroed, 1)
            wait_drained(pool, "meta")
            pool.wait_ge(table_ready, 1)

            g.memset(passed, 0.0).then_inc(passed_ready, 1)
            with pool.Fori(0, E) as e:
                extra = pool.value_load(meta_i[0:1, bass.ds(e, 1)], min_val=0, max_val=T // CAP - 1)
                first = pool.value_load(meta_i[0:1, bass.ds(e + E, 1)], min_val=0, max_val=E + T * TOPK // CAP)
                pool.wait_ge(passed_ready, first + e + 1)
                g.tensor_tensor(passed, cap_row, cap_row, ALU.subtract).then_inc(passed_ready, 1)
                with pool.Fori(0, pool.snap(extra + 1)) as r:
                    b = pool.snap(first + r)
                    pool.wait_ge(pt_full, b + 1)
                    pool.wait_ge(passed_ready, e + b + 2)
                    g.tensor_tensor(cols, table[:, bass.ds(e * 4, 4)], passed, ALU.subtract).then_inc(cols_ready, 1)
                    pool.wait_ge(cols_ready, b + 1)
                    g.tensor_tensor(passed, passed, cap_row, ALU.add).then_inc(passed_ready, 1)
            last_b = pool.value_load(meta_i[0:1, 2 * E - 1:2 * E], min_val=0, max_val=E + T * TOPK // CAP)
            last_r = pool.value_load(meta_i[0:1, E - 1:E], min_val=0, max_val=T // CAP - 1)
            blocks = pool.snap(last_b + last_r + 1)
            pool.wait_ge(pt_full, blocks + 1)
            pool.wait_ge(passed_ready, blocks + E + 1)
            g.tensor_tensor(cols, passed, cap_row, ALU.add).then_inc(cols_ready, 1)

        N_CONST = 9 + 17 + 1 + 3 + 2

        @block.scalar
        def _(act):
            a = nc.scalar
            chain = [0]

            def link(ins):
                chain[0] += 1
                ins.then_inc(a_chain, 1)
                act.wait_ge(a_chain, chain[0])

            def root(dst, src, n):
                a.activation(dst, src, ACT.Sqrt, bias=eps[:, 0:1], scale=1.0 / n).then_inc(root_ready, 1)

            def drain(job, ins):
                ins.then_inc(drained["a"], 1)

            act.wait_ge(const_ready, 1)
            a.activation(scrap[:, 0:1], eps[:, 0:1], ACT.Sqrt)
            for i in range(TT):
                act.wait_ge(loaded[f"x{i}"], 16)
                a.activation(hT[:, 4 * i:4 * i + 4].rearrange("p k q -> p (k q)"), xs[:, i, :], ACT.Square,
                             accum_out=stat[:, i:i + 1]).then_inc(x_squares, 1)
            act.wait_ge(x_squares, TT)
            root(roots[:, 0:2], stat[:, 0:2], D)
            act.wait_ge(loaded["mem"], 16)
            for i in range(TT):
                a.activation(memn[:, i].rearrange("p k q -> p (k q)"), mem_sb[:, i, :], ACT.Square,
                             accum_out=stat[:, 2 + i:3 + i]).then_inc(m_squares, 1)
            act.wait_ge(m_squares, TT)
            root(roots[:, 2:4], stat[:, 2:4], D)
            act.wait_ge(trig_arg, 2)
            a.activation(trig, ttmp[:, 2:4], ACT.Sin).then_inc(trig_ready, 1)
            wait_drained(act, "u1")
            for i in range(TT):
                a.activation(krowsq(i), u_tok[:, i, 0:Q_LORA], ACT.Square,
                             accum_out=stat[:, 4 + i:5 + i]).then_inc(cq_squares, 1)
            for i in range(TT):
                a.activation(krowsq(2 + i)[:, 0:KV_LORA], u_tok[:, i, Q_LORA:Q_LORA + KV_LORA], ACT.Square,
                             accum_out=stat[:, 6 + i:7 + i]).then_inc(cq_squares, 1)
            def gate_job(c):
                job = f"cv{c}"
                wait_full(act, job)
                if c >= 2:
                    wait_drained(act, f"cv{c - 2}")
                a.activation(sg[:, c % 2, :], bank_of(job)[:, T:2 * T], ACT.Sigmoid).then_inc(gate_sig, 1)

            gate_job(0)
            gate_job(1)
            wait_drained(act, "vec")
            for i in range(4):
                job = f"mT{i}"
                wait_full(act, job)
                b = bank_of(job)
                link(a.activation(mT[:, 2 * i, :], b[:, 0:T], ACT.Copy, scale=gm_sb[:, 2 * i:2 * i + 1]))
                drain(job, a.activation(mT[:, 2 * i + 1, :], b[:, T:2 * T], ACT.Copy,
                                        scale=gm_sb[:, 2 * i + 1:2 * i + 2]))
            gate_job(2)
            gate_job(3)
            act.wait_ge(cq_squares, 4)
            root(roots[:, 4:6], stat[:, 4:6], Q_LORA)
            root(roots[:, 6:8], stat[:, 6:8], KV_LORA)
            def key_job(i):
                job = f"xk{i}"
                wait_full(act, job)
                drain(job, a.activation(kTm[:, 2 * i:2 * i + 2, :].rearrange("p k m -> p (k m)"),
                                        bank_of(job)[:, :], ACT.Copy))

            def value_job(i):
                job = f"xv{i}"
                n, t = divmod(i, 2)
                wait_full(act, job)
                drain(job, a.activation(vm[:, n, t * BANK:(t + 1) * BANK], bank_of(job)[:, :], ACT.Copy))

            key_job(0)
            key_job(1)
            wait_full(act, "krT")
            drain("krT", a.activation(KTs[NOPE:QK, :, :],
                                      bank_of("krT")[NOPE:QK, 0:T].unsqueeze(1).broadcast_to([ROPE, HEADS, T]), ACT.Copy))
            for t in range(TT):
                for h in range(2):
                    job = f"q{t}{h}"
                    wait_full(act, job)
                    drain(job, a.activation(q_tok[:, t, 4 * h:4 * h + 4, :].rearrange("p h n -> p (h n)"),
                                            bank_of(job)[:, 0:4 * QK], ACT.Copy))
            for i in range(4):
                job = f"kn{i}"
                wait_full(act, job)
                drain(job, a.activation(KTs[0:NOPE, 2 * i:2 * i + 2, :].rearrange("p h t -> p (h t)"),
                                        bank_of(job)[0:NOPE, :], ACT.Copy))
            for t in range(TT):
                job = f"v{t}"
                wait_full(act, job)
                drain(job, a.activation(Vs[:, t, :], bank_of(job)[:, :], ACT.Copy))

            for i in range(4):
                job = f"qT{i}"
                wait_full(act, job)
                drain(job, a.activation(qTs[0:QK, 2 * i:2 * i + 2, :].rearrange("p h t -> p (h t)"),
                                        bank_of(job)[0:QK, :], ACT.Copy))
            act.wait_ge(s_ready, 1)
            a.activation(part("S0"), part("S0"), ACT.Exp, scale=float(QK) ** -0.5).then_inc(e_ready, 1)
            act.wait_ge(s_ready, 2)
            a.activation(part("S1"), part("S1"), ACT.Exp, scale=float(QK) ** -0.5).then_inc(e_ready, 1)
            key_job(2)
            key_job(3)
            for i in range(2):
                job = f"pT0{i}"
                wait_full(act, job)
                drain(job, a.activation(PT0[:, 4 * i:4 * i + 4, :].rearrange("p h q -> p (h q)"),
                                        bank_of(job)[:, :], ACT.Copy))
            for i in range(4):
                job = f"pT1{i}"
                wait_full(act, job)
                drain(job, a.activation(PT1[:, 2 * i:2 * i + 2].rearrange("p h a q -> p (h a q)"),
                                        bank_of(job)[:, :], ACT.Copy))
            value_job(0)
            wait_drained(act, "mean")
            a.activation(sq4, acc, ACT.Square).then_inc(zsq_ready, 1)
            a.activation(scrap[:, 3:4], eps[:, 0:1], ACT.Sqrt)
            wait_full(act, "var")
            root(rstd_t, bank_of("var")[:, 0:T], 1)
            act.wait_ge(ln_ready, CT)
            a.activation(sq4, acc, ACT.Sigmoid).then_inc(lnsig_ready, 1)
            value_job(1)
            value_job(2)
            for t in range(TT):
                wait_drained(act, f"w{t}1")
                a.activation(slab(13)[:, t * D:(t + 1) * D], xs[:, t, :], ACT.Square,
                             accum_out=stat[:, 8 + t:9 + t]).then_inc(x1_squares, 1)
            act.wait_ge(x1_squares, TT)
            root(roots[:, 8:10], stat[:, 8:10], D)
            for i in range(4):
                job = f"xq{i}"
                wait_full(act, job)
                drain(job, a.activation(qT2[:, 2 * i:2 * i + 2, :].rearrange("p k t -> p (k t)"),
                                        bank_of(job)[:, :], ACT.Copy))
            act.wait_ge(x1_scale, 1)
            for t in range(TT):
                wait_drained(act, f"xs{t}1")
                v = px[:, t].rearrange("p h m -> p (h m)")
                a.activation(v, v, ACT.Exp, scale=stat[:, 8 + t:9 + t]).then_inc(xe_ready, 1)
            value_job(3)
            for t in range(TT):
                for g in range(2):
                    job = f"xp{t}{g}"
                    wait_full(act, job)
                    drain(job, a.activation(ptx[:, 2 * g:2 * g + 2, :, t * P:(t + 1) * P],
                                            bank_of(job)[:, :].rearrange("p (h a q) -> p h a q", h=2, a=2), ACT.Copy))
            for i in range(4):
                job = f"xo{i}"
                wait_full(act, job)
                drain(job, a.activation(oT2[:, 2 * i:2 * i + 2, :].rearrange("p k t -> p (k t)"),
                                        bank_of(job)[:, :], ACT.Copy))
            a.activation(scrap[:, 1:2], eps[:, 0:1], ACT.Sqrt)
            for t in range(TT):
                wait_drained(act, f"wo{t}1")
                a.activation(rows[:, t].rearrange("p k q -> p (k q)"), xs[:, t, :], ACT.Square,
                             accum_out=stat[:, 10 + t:11 + t]).then_inc(x2_squares, 1)
            act.wait_ge(x2_squares, TT)
            root(roots[:, 10:12], stat[:, 10:12], D)
            a.activation(scrap[:, 2:3], eps[:, 0:1], ACT.Exp)
            act.wait_ge(x2_scale, 1)
            for t in range(TT):
                a.activation(rows[:, t].rearrange("p k q -> p (k q)"), xs[:, t, :], ACT.Copy,
                             scale=stat[:, 10 + t:11 + t]).then_inc(rows_normed, 1)
            act.wait_ge(top_ready, 1)
            a.activation(stat[:, 16:16 + TT * TOPK], stat[:, 16:16 + TT * TOPK], ACT.Exp).then_inc(topexp_ready, 1)

            wait_full(act, "gT")
            a.activation(PT2[:, 0:P], bank_of("gT")[:, 0:P], ACT.Copy).then_inc(pt_copied, 1)
            drain("gT", a.activation(PT2[:, P:T], bank_of("gT")[:, P:T], ACT.Copy))
            a.activation(scrap[:, 0:1], eps[:, 0:1], ACT.Copy).then_inc(y_ready, 1)
            wait_drained(act, "meta")

            def gathered(b):
                act.wait_ge(g_full, b + 1)
                a.activation(G_sb, banks[4][:, :], ACT.Copy).then_inc(g_copied, 1)

            def gathered_columns(b):
                act.wait_ge(x_full, b + 1)
                a.activation(xg.rearrange("p (h c) s -> p c h s", h=2),
                             banks[2][:, :].rearrange("p (c h s) -> p c h s", c=4, h=2), ACT.Copy).then_inc(xg_ready, 1)

            gathered(0)
            gathered_columns(0)
            with act.Fori(0, E) as e:
                extra = act.value_load(meta_i[0:1, bass.ds(e, 1)], min_val=0, max_val=T // CAP - 1)
                first = act.value_load(meta_i[0:1, bass.ds(e + E, 1)], min_val=0, max_val=E + T * TOPK // CAP)
                with act.Fori(0, act.snap(extra + 1)) as r:
                    b = act.snap(first + r)
                    a.activation(scrap[:, 3:4], eps[:, 0:1], ACT.Sigmoid)
                    act.wait_ge(up_steps, b * KT + KT)
                    a.activation(U_sb[:, :, 0:64].rearrange("p j q -> p q j"),
                                 banks[0][:, :].rearrange("p (q j) -> p q j", j=KT), ACT.Copy).then_inc(u_by_a, 1)
                    for i in range(2):
                        act.wait_ge(glu_ready, b * 2 + (i + 1))
                        a.activation(sig[:, 4 * i:4 * i + 4, :], A_sb[:, 4 * i:4 * i + 4, 0, :], ACT.Sigmoid,
                                     scale=ALPHA).then_inc(sig_ready, 1)
                    act.wait_ge(pt_full, b + 2)
                    a.activation(PT2[:, :], banks[6][:, 0:T], ACT.Copy)
                    a.activation(gslot, banks[6][:, T:T + 1], ACT.Copy).then_inc(pt_copied, 1)
                    gathered(b + 1)
                    gathered_columns(b + 1)
                    act.wait_ge(down_steps, b * 4 + 4)
                    act.wait_ge(pt_copied, b + 2)
                    a.activation(y_sb, banks[5][:, :], ACT.Copy, scale=gslot).then_inc(y_ready, 1)
            last_b = act.value_load(meta_i[0:1, 2 * E - 1:2 * E], min_val=0, max_val=E + T * TOPK // CAP)
            last_r = act.value_load(meta_i[0:1, E - 1:E], min_val=0, max_val=T // CAP - 1)
            a.activation(scrap[:, 1:2], eps[:, 0:1], ACT.Sqrt)
            for t in range(TT):
                act.wait_ge(y_added, act.snap((last_b + last_r) * 4 + (7 + 2 * t)))
                a.activation(buf_f[:, t * D:(t + 1) * D], xs[:, t, :], ACT.Square,
                             accum_out=stat[:, 12 + t:13 + t]).then_inc(fin_squares, 1)
                act.wait_ge(fin_squares, t + 1)
                root(roots[:, 12 + t:13 + t], stat[:, 12 + t:13 + t], D)

        @block.vector
        def _(dve):
            v = nc.vector
            chain = [0]

            def link(ins):
                chain[0] += 1
                ins.then_inc(v_chain, 1)
                dve.wait_ge(v_chain, chain[0])

            def rstd(name, c, n, tiles=TT, ready=None):
                wait_root(dve, name)
                r, ms, q = roots[:, c:c + tiles], stat[:, c:c + tiles], newton[:, 0:tiles]
                link(v.reciprocal(r, r))
                link(v.tensor_scalar(ms, ms, 1.0 / n, EPS, ALU.mult, ALU.add))
                link(v.tensor_tensor(q, r, r, ALU.mult))
                link(v.tensor_tensor(q, q, ms, ALU.mult))
                link(v.tensor_scalar(q, q, -0.5, 1.5, ALU.mult, ALU.add))
                ins = v.tensor_tensor(ms, r, q, ALU.mult)
                if ready is None:
                    link(ins)
                else:
                    ins.then_inc(ready, 1)
                    dve.wait_ge(ready, 1)

            def free(job, ins):
                ins.then_inc(drained["v"], 1)

            def bc(ap, n):
                return ap.unsqueeze(2).broadcast_to([ap.shape[0], ap.shape[1], n])

            rstd("x", 0, D)
            for t in range(TT):
                v.tensor_scalar(xn[:, t].rearrange("p k q -> p (k q)"), xs[:, t, :], stat[:, t:t + 1], None,
                                ALU.mult).then_inc(xn_ready, 1)
            wait_full(dve, "vec")
            b = bank_of("vec")
            link(v.tensor_copy(taps[:, :], b[:, 0:TAPS * CT]))
            free("vec", v.tensor_copy(vecs[:, :], b[:, P:P + NVEC]))
            wait_drained(dve, "vec")
            for i in range(4):
                job = f"hT{i}"
                wait_full(dve, job)
                free(job, v.tensor_tensor(hT[:, 2 * i:2 * i + 2, :], bank_of(job)[:, :].rearrange("p (k t) -> p k t", k=2),
                                          bc(gmix_sb[:, 2 * i:2 * i + 2], T), ALU.mult))
            dve.wait_ge(loaded["pos"], 16)
            dve.wait_ge(const_ready, 19)
            link(v.tensor_copy(pos_f, pos_i))
            ang = ttmp[:, 0]
            for t in range(TT):
                link(v.tensor_scalar(ang[:, t, :], freq, pos_f[:, t:t + 1], None, ALU.mult))
            ROUND = 12582912.0
            two_pi = 2 * np.pi
            c1 = float(np.float32(6.28125))
            c2 = float(np.float32(np.round((two_pi - c1) * 2 ** 22) / 2 ** 22))
            c3 = float(two_pi - c1 - c2)
            for f, quarter in ((0, 0.25), (1, 0.0)):
                k, r = ttmp[:, 1], ttmp[:, 2 + f]
                link(v.tensor_scalar(k, ang, 1.0 / two_pi, quarter, ALU.mult, ALU.add))
                link(v.tensor_scalar(k, k, ROUND, None, ALU.add))
                link(v.tensor_scalar(k, k, ROUND, None, ALU.subtract))
                link(v.scalar_tensor_tensor(r, k, -c1, ang, ALU.mult, ALU.add))
                link(v.scalar_tensor_tensor(r, k, -c2, r, ALU.mult, ALU.add))
                link(v.scalar_tensor_tensor(r, k, -c3, r, ALU.mult, ALU.add))
                if f == 0:
                    link(v.tensor_scalar(r, r, float(np.pi / 2), None, ALU.add))
                v.tensor_scalar(r, r, 3.1415925, -3.1415925, ALU.min, ALU.max).then_inc(trig_arg, 1)
                dve.wait_ge(trig_arg, f + 1)
            dve.wait_ge(const_ready, N_CONST)
            rstd("mem", 2, D)
            for t in range(TT):
                v.tensor_scalar(memn[:, t].rearrange("p k q -> p (k q)"), mem_sb[:, t, :], stat[:, 2 + t:3 + t], None,
                                ALU.mult).then_inc(memn_ready, 1)
            for t in range(TT):
                wait_full(dve, f"u{t}")
                free(f"u{t}", v.tensor_copy(u_tok[:, t, :], bank_of(f"u{t}")[:, 0:TOK_COLS]))
            wait_drained(dve, "u1")
            dve.wait_ge(trig_ready, 1)

            def rotate(out1, out2, x1, x2, cos, sin, tmp):
                link(v.tensor_tensor(tmp[0], x1, cos, ALU.mult))
                link(v.tensor_tensor(tmp[1], x2, sin, ALU.mult))
                link(v.tensor_tensor(tmp[2], x1, sin, ALU.mult))
                link(v.tensor_tensor(tmp[3], x2, cos, ALU.mult))
                link(v.tensor_tensor(out1, tmp[0], tmp[1], ALU.subtract))
                return v.tensor_tensor(out2, tmp[2], tmp[3], ALU.add)

            o3 = Q_LORA + KV_LORA
            rotate(krow[:, :, NOPE:NOPE + 16], krow[:, :, NOPE + 16:QK], u_tok[:, :, o3:o3 + 16],
                   u_tok[:, :, o3 + 16:o3 + 32], trig[:, 0], trig[:, 1],
                   [ktmp[:, i] for i in range(4)]).then_inc(krow_ready, 1)
            for c in range(CT):
                dve.wait_ge(gate_sig, c + 1)
                free(f"cv{c}", v.tensor_tensor(z[:, c, TAPS - 1:], bank_of(f"cv{c}")[:, 0:T], sg[:, c % 2, :], ALU.mult))
            rstd("cq", 4, Q_LORA)
            rstd("ckv", 6, KV_LORA)
            for t in range(TT):
                cq, ckv = u_tok[:, t, 0:Q_LORA], u_tok[:, t, Q_LORA:o3]
                v.tensor_scalar(cq, cq, stat[:, 4 + t:5 + t], None, ALU.mult).then_inc(cq_ready, 1)
                v.tensor_scalar(ckv, ckv, stat[:, 6 + t:7 + t], None, ALU.mult).then_inc(cq_ready, 1)
            conv_n = [0]

            def conv_taps(ws):
                for w in ws:
                    for c in range(CONV_V):
                        n = conv_n[0]
                        if n >= CONV_V:
                            dve.wait_ge(conv_step, n - CONV_V + 1)
                        src, wt = z[:, c, w:w + T], taps[:, w * CT + c:w * CT + c + 1]
                        if w == 0:
                            ins = v.tensor_scalar(acc[:, c, :], src, wt, vecs[:, c:c + 1], ALU.mult, ALU.add)
                        else:
                            ins = v.scalar_tensor_tensor(acc[:, c, :], src, wt, acc[:, c, :], ALU.mult, ALU.add)
                        ins.then_inc(conv_step, 1)
                        conv_n[0] += 1

            wait_drained(dve, "cv3")
            conv_taps(range(0, 10))
            wait_full(dve, "cqT")
            free("cqT", v.tensor_tensor(cqT, bank_of("cqT")[:, :].rearrange("p (k t) -> p k t", k=2),
                                        bc(vecs[:, 12:14], T), ALU.mult))
            wait_full(dve, "ckvT")
            free("ckvT", v.tensor_scalar(ckvT, bank_of("ckvT")[:, 0:T], vecs[:, 14:15], None, ALU.mult))
            for t in range(TT):
                wait_drained(dve, f"q{t}1")
                cos = trig[:, 0, t, :].unsqueeze(1).broadcast_to([P, HEADS, 16])
                sin = trig[:, 1, t, :].unsqueeze(1).broadcast_to([P, HEADS, 16])
                x1, x2 = q_tok[:, t, :, NOPE:NOPE + 16], q_tok[:, t, :, NOPE + 16:QK]
                rotate(x1, x2, x1, x2, cos, sin, [rtmp[:, i] for i in range(4)]).then_inc(q_ready, 1)

            conv_taps(range(10, 13))
            mx, sm = stat[:, 24:32], stat[:, 32:48]
            for t, S, keys, per in ((0, S0, P, 4), (1, S1, T, 2)):
                for i in range(HEADS // per):
                    job = f"s{t}{i}"
                    wait_full(dve, job)
                    m = mask[:, t, 0:keys].unsqueeze(1).broadcast_to([P, per, keys])
                    free(job, v.tensor_tensor(S[:, per * i:per * i + per, :],
                                              bank_of(job)[:, :].rearrange("p (h k) -> p h k", h=per), m, ALU.add))
                wait_drained(dve, f"s{t}{HEADS // per - 1}")
                link(v.tensor_reduce(mx, S, AX.X, ALU.max))
                v.tensor_tensor(S, S, bc(mx, keys), ALU.subtract).then_inc(s_ready, 1)
            for t, S in ((0, S0), (1, S1)):
                dve.wait_ge(e_ready, t + 1)
                link(v.tensor_reduce(sm[:, 8 * t:8 * t + 8], S, AX.X, ALU.add))
            link(v.reciprocal(sm, sm))
            conv_taps(range(13, 24))
            for t in range(TT):
                wait_full(dve, f"o{t}")
                free(f"o{t}", v.tensor_tensor(o_tok[:, t, :].rearrange("p (h n) -> p h n", h=HEADS),
                                              bank_of(f"o{t}")[:, :].rearrange("p (h n) -> p h n", h=HEADS),
                                              bc(sm[:, 8 * t:8 * t + 8], VDIM), ALU.mult))
            for t in range(TT):
                wait_full(dve, f"oT{t}")
                free(f"oT{t}", v.tensor_copy(yT[:, 0:4, t * P:(t + 1) * P],
                                             bank_of(f"oT{t}")[:, :].rearrange("p (k q) -> p k q", k=4)))
            conv_taps(range(24, TAPS))
            dve.wait_ge(conv_step, conv_n[0])
            wait_full(dve, "mean")
            free("mean", v.tensor_tensor(acc, acc, bank_of("mean")[:, 0:T].unsqueeze(1).broadcast_to([P, CT, T]), ALU.subtract))
            wait_drained(dve, "mean")
            wait_root(dve, "var")
            link(v.reciprocal(rstd_t, rstd_t))
            q = part("PT0")[:, 0:T]
            link(v.tensor_tensor(q, rstd_t, rstd_t, ALU.mult))
            free("var", v.scalar_tensor_tensor(q, bank_of("var")[:, 0:T], EPS, q, ALU.add, ALU.mult))
            wait_drained(dve, "var")
            link(v.tensor_scalar(q, q, -0.5, 1.5, ALU.mult, ALU.add))
            link(v.tensor_tensor(rstd_t, rstd_t, q, ALU.mult))
            link(v.tensor_tensor(acc, acc, rstd_t.unsqueeze(1).broadcast_to([P, CT, T]), ALU.mult))
            for c in range(CT):
                v.tensor_scalar(acc[:, c, :], acc[:, c, :], vecs[:, 4 + c:5 + c], vecs[:, 8 + c:9 + c],
                                ALU.mult, ALU.add).then_inc(ln_ready, 1)
            dve.wait_ge(lnsig_ready, 1)
            v.tensor_tensor(yT[:, 4:8, :], acc, sq4, ALU.mult).then_inc(yconv_ready, 1)
            def channels(jobs, t, dst, gain):
                for i in range(2):
                    job = f"{jobs}{t}{i}"
                    wait_full(dve, job)
                    free(job, v.tensor_tensor(dst[:, 4 * i:4 * i + 4, t * P:(t + 1) * P],
                                              bank_of(job)[:, :].rearrange("p (k t) -> p k t", k=4),
                                              bc(gain[:, 4 * i:4 * i + 4], P), ALU.mult))

            for t in range(TT):
                for n in range(2):
                    job = f"w{t}{n}"
                    wait_full(dve, job)
                    s = xs[:, t, n * BANK:(n + 1) * BANK]
                    free(job, v.tensor_tensor(s, bank_of(job)[:, :], s, ALU.add))
            channels("h2T", 0, h2T, gx_sb)
            channels("h2T", 1, h2T, gx_sb)
            rstd("x1", 8, D)
            v.tensor_scalar(stat[:, 8:10], stat[:, 8:10], float(XD) ** -0.5, None, ALU.mult).then_inc(x1_scale, 1)
            for t in range(TT):
                for g in range(2):
                    job = f"xs{t}{g}"
                    wait_full(dve, job)
                    bk = bank_of(job)[:, :].rearrange("p (h m) -> p h m", h=2)
                    m2 = mx[:, 2 * g:2 * g + 2]
                    link(v.tensor_reduce(m2, bk, AX.X, ALU.max))
                    free(job, v.tensor_tensor(px[:, t, 2 * g:2 * g + 2, :], bk, bc(m2, M), ALU.subtract))
            for t in range(TT):
                dve.wait_ge(xe_ready, t + 1)
                s4 = sm[:, 4 * t:4 * t + 4]
                link(v.tensor_reduce(s4, px[:, t], AX.X, ALU.add))
                link(v.reciprocal(s4, s4))
                v.tensor_tensor(px[:, t], px[:, t], bc(s4, M), ALU.mult).then_inc(px_ready, 1)
            for t in range(TT):
                for n in range(2):
                    job = f"wo{t}{n}"
                    wait_full(dve, job)
                    s = xs[:, t, n * BANK:(n + 1) * BANK]
                    free(job, v.tensor_tensor(s, bank_of(job)[:, :], s, ALU.add))
            channels("tT", 0, tT, gf_sb)
            channels("tT", 1, tT, gf_sb)
            rstd("x2", 10, D, ready=x2_scale)
            lg = rt[:, 0:2 * E].rearrange("p (a e) -> p a e", a=TT)
            pick = rt[:, 64:128].rearrange("p (a e) -> p a e", a=TT)
            top8 = rt[:, 192:208].rearrange("p (a j) -> p a j", a=TT)
            idx_u = rt[:, 208:224].bitcast(u32).rearrange("p (a j) -> p a j", a=TT)
            idx_f = rt[:, 224:240].rearrange("p (a j) -> p a j", a=TT)
            tsum = rt[:, 306:308]
            count = rt[:, 308:309]
            rounds_c = rt[:, 309:310]
            step = rt[:, 310:311]
            hit = rt[:, 512:768].rearrange("p (a j e) -> p a j e", a=TT, j=TOPK)
            gate = gates2[:, :, 0:E]
            top4 = stat[:, 16:16 + TT * TOPK].rearrange("p (a j) -> p a j", a=TT)
            dve.wait_ge(loaded["router"], 32)
            for t in range(TT):
                job = f"lg{t}"
                wait_full(dve, job)
                free(job, v.scalar_tensor_tensor(lg[:, t, :], bank_of(job)[:, 0:E], stat[:, 10 + t:11 + t],
                                                 br_sb[:, :], ALU.mult, ALU.add))
                wait_drained(dve, job)
                link(v.max(top8[:, t, :], lg[:, t, :]))
                link(v.max_index(idx_u[:, t, :], top8[:, t, :], lg[:, t, :]))
                if t == TT - 1:
                    v.tensor_tensor(top4, top8[:, :, 0:TOPK], top8[:, :, 0:1].broadcast_to([P, TT, TOPK]),
                                    ALU.subtract).then_inc(top_ready, 1)
                link(v.tensor_copy(idx_f[:, t, 0:TOPK], idx_u[:, t, 0:TOPK]))
                link(v.tensor_tensor(hit[:, t], e_row[:, :].unsqueeze(1).broadcast_to([P, TOPK, E]),
                                     bc(idx_f[:, t, 0:TOPK], E), ALU.is_equal))
                v.tensor_reduce(pick[:, t, :], hit[:, t].rearrange("p j e -> p e j"), AX.X, ALU.add).then_inc(picks_ready, 1)
            wait_full(dve, "count")
            link(v.tensor_copy(count[0:E, :], bank_of("count")[0:E, 0:1]))
            link(v.tensor_scalar(rounds_c[0:E, :], count[0:E, :], float(CAP), 1.0, ALU.is_gt, ALU.add))
            for j in range(2, T // CAP):
                link(v.tensor_scalar(step[0:E, :], count[0:E, :], float(j * CAP), None, ALU.is_gt))
                link(v.tensor_tensor(rounds_c[0:E, :], rounds_c[0:E, :], step[0:E, :], ALU.add))
            free("count", v.tensor_copy(count[0:E, :], rounds_c[0:E, :]))
            wait_full(dve, "rank")
            dve.wait_ge(picks_ready, 2)
            pos_v = tab4[:, :, 0:2].rearrange("p e a -> p a e")
            gate_v = tab4[:, :, 2:4].rearrange("p e a -> p a e")
            link(v.scalar_tensor_tensor(pos_v, bank_of("rank")[:, 0:2 * E].rearrange("p (a e) -> p a e", a=TT),
                                        ABSENT, pick, ALU.add, ALU.mult))
            free("rank", v.tensor_scalar(pos_v, pos_v, ABSENT, None, ALU.subtract))
            wait_drained(dve, "rank")
            for t in range(TT):
                v.tensor_scalar(P2v[:, t, :], slot_row[:, :], tab4[:, 0, t:t + 1], None, ALU.is_equal).then_inc(p2_ready, 1)
            dve.wait_ge(topexp_ready, 1)
            dve.wait_ge(cap_set, 3)
            link(v.tensor_reduce(tsum, top4, AX.X, ALU.add))
            link(v.reciprocal(tsum, tsum))
            link(v.tensor_tensor(top4, top4, bc(tsum, TOPK), ALU.mult))
            for t in range(TT):
                ins = v.tensor_tensor(hit[:, t], hit[:, t], bc(top4[:, t, :], E), ALU.mult)
                if t == TT - 1:
                    link(ins)
                else:
                    ins.then_inc(top_ready, 1)
            dve.wait_ge(top_ready, 2)
            wait_full(dve, "meta")
            link(v.tensor_scalar(meta_i[0:1, 0:E], bank_of("meta")[0:1, 0:E], 1.0, None, ALU.subtract))
            free("meta", v.tensor_copy(meta_i[0:1, E:2 * E], bank_of("meta")[0:1, E:2 * E]))
            link(v.tensor_reduce(gate, hit.rearrange("p a j e -> p a e j"), AX.X, ALU.add))
            v.tensor_copy(gate_v, gate).then_inc(table_ready, 1)
            v.tensor_copy(gates2[:, :, 64:64 + E], gate).then_inc(gates_ready, 1)
            v.tensor_copy(newton[:, 0:1], eps[:, 0:1]).then_inc(y_added, 1)
            wait_drained(dve, "meta")
            dve.wait_ge(loaded["bup"], 32)

            def add_up(b):
                for t in range(TT):
                    for n in range(2):
                        dve.wait_ge(c_full, b * 4 + (2 * t + n + 1))
                        s = xs[:, t, n * BANK:(n + 1) * BANK]
                        v.tensor_tensor(s, banks[COMBINE[2 * t + n]][:, :], s, ALU.add).then_inc(y_added, 1)

            def onehot(b):
                dve.wait_ge(pt_full, b + 1)
                dve.wait_ge(cols_ready, b + 1)
                for t in range(TT):
                    v.tensor_scalar(P2v[:, t, :], slot_row[:, :], cols[:, t:t + 1], None, ALU.is_equal).then_inc(p2_ready, 1)

            with dve.Fori(0, E) as e:
                extra = dve.value_load(meta_i[0:1, bass.ds(e, 1)], min_val=0, max_val=T // CAP - 1)
                first = dve.value_load(meta_i[0:1, bass.ds(e + E, 1)], min_val=0, max_val=E + T * TOPK // CAP)
                v.tensor_copy(bcol, bup_sb[:, bass.ds(e * (2 * KT), 2 * KT)]).then_inc(bcol_ready, 1)
                with dve.Fori(0, dve.snap(extra + 1)) as r:
                    b = dve.snap(first + r)
                    dve.wait_ge(up_steps, b * KT + KT)
                    v.tensor_copy(U_sb[:, :, 64:128].rearrange("p j q -> p q j"),
                                  banks[1][:, :].rearrange("p (q j) -> p q j", j=KT)).then_inc(u_by_v, 1)
                    add_up(b)
                    dve.wait_ge(bcol_ready, e + 1)
                    for i in range(2):
                        js = slice(4 * i, 4 * i + 4)
                        dve.wait_ge(t_full, b * 2 + (i + 1))
                        bias = bcol2[:, :, js].rearrange("p h j -> p j h").unsqueeze(3).broadcast_to([P, 4, 2, CAP])
                        v.tensor_tensor(A_sb[:, js], banks[2 + i][:, :].rearrange("p (j h t) -> p j h t", j=4, h=2),
                                        bias, ALU.add).then_inc(biased, 1)
                        dve.wait_ge(biased, b * 2 + (i + 1))
                        glu, lin = A_sb[:, js, 0, :], A_sb[:, js, 1, :]
                        v.tensor_scalar(glu, glu, LIMIT, None, ALU.min).then_inc(glu_ready, 1)
                        v.tensor_scalar(lin, lin, LIMIT, -LIMIT, ALU.min, ALU.max).then_inc(lin_ready, 1)
                        dve.wait_ge(glu_ready, b * 2 + (i + 1))
                        dve.wait_ge(lin_ready, b * 2 + (i + 1))
                        v.scalar_tensor_tensor(lin, lin, 1.0, glu, ALU.add, ALU.mult).then_inc(prod_ready, 1)
                        dve.wait_ge(prod_ready, b * 2 + (i + 1))
                        dve.wait_ge(sig_ready, b * 2 + (i + 1))
                        v.tensor_tensor(actT[:, js, :], lin, sig[:, js, :], ALU.mult).then_inc(act_ready, 1)
                    onehot(b + 1)
            last_b = dve.value_load(meta_i[0:1, 2 * E - 1:2 * E], min_val=0, max_val=E + T * TOPK // CAP)
            last_r = dve.value_load(meta_i[0:1, E - 1:E], min_val=0, max_val=T // CAP - 1)
            add_up(dve.snap(last_b + last_r + 1))
            for t in range(TT):
                rstd(f"out{t}", 12 + t, D, 1)
                v.scalar_tensor_tensor(xs[:, t, :], xs[:, t, :], stat[:, 12 + t:13 + t], gfin, ALU.mult,
                                       ALU.mult).then_inc(fin_ready, 1)

        @block.tensor
        def _(pe):
            t_ = nc.tensor

            def begin(job):
                i = job_at[job]
                if i >= 8:
                    wait_drained(pe, JOBS[i - 8][0])
                return bank_of(job)

            def end(job, ins):
                ins.then_inc(full[full_at[job][0]], 1)

            def transposes(jobs, src, some=range(4)):
                for i in some:
                    b = begin(f"{jobs}{i}")
                    for k in range(2):
                        for a in range(TT):
                            ins = t_.transpose(b[:, k * T + a * P:k * T + (a + 1) * P], src[:, a, 2 * i + k, :], ident[:, :])
                    end(f"{jobs}{i}", ins)

            pe.wait_ge(const_ready, 3)
            pe.wait_ge(loaded["vrow1"], 16)
            pe.wait_ge(loaded["vrow2"], 16 * 9)
            b = begin("vec")
            t_.transpose(b[:, 0:TAPS * CT], vrow1[0:TAPS * CT, :], ident[0:TAPS * CT, 0:TAPS * CT])
            end("vec", t_.transpose(b[:, P:P + NVEC], vrow2[0:NVEC, :], ident[0:NVEC, 0:NVEC]))
            pe.wait_ge(xn_ready, TT)
            transposes("hT", xn, range(2))
            ub = [begin(f"u{t}") for t in range(TT)]
            cb = [begin(f"cv{c}") for c in range(CT)]
            for k in range(KT):
                if k in (1, 3):
                    transposes("hT", xn, [2 + k // 2])
                wait_drained(pe, f"hT{k // 2}")
                pe.wait_ge(loaded[f"win{k // 2}"], 16)
                first, last = k == 0, k == KT - 1
                for t in range(TT):
                    ins = t_.matmul(ub[t][:, 0:TOK_COLS], hT[:, k, t * P:(t + 1) * P], w_in_sb[:, k, 0:TOK_COLS],
                                    start=first, stop=last)
                    if last:
                        end(f"u{t}", ins)
                for c in range(CT):
                    for g in range(2):
                        at = TOK_COLS + g * CONV + c * P
                        ins = t_.matmul(cb[c][:, g * T:(g + 1) * T], w_in_sb[:, k, at:at + P], hT[:, k, :],
                                        start=first and g == 0, stop=last and g == 1)
                    if last:
                        end(f"cv{c}", ins)
            pe.wait_ge(memn_ready, TT)
            transposes("mT", memn)

            def key_job(i):
                b = begin(f"xk{i}")
                for j in range(2):
                    for k in range(KT):
                        pe.wait_ge(loaded[f"wk{k // 4}"], 16)
                        at = (2 * i + j) * P
                        ins = t_.matmul(b[:, j * M:(j + 1) * M], wk_sb[:, k, at:at + P], mT[:, k, :],
                                        start=k == 0, stop=k == KT - 1)
                end(f"xk{i}", ins)

            def value_job(i):
                b = begin(f"xv{i}")
                a, n = divmod(i, 2)
                pe.wait_ge(loaded["wv"], 16)
                for k in range(KT):
                    ins = t_.matmul(b[:, :], mT[:, k, a * P:(a + 1) * P], wv_sb[:, k, n * BANK:(n + 1) * BANK],
                                    start=k == 0, stop=k == KT - 1)
                end(f"xv{i}", ins)

            wait_drained(pe, "mT3")
            key_job(0)
            key_job(1)
            pe.wait_ge(cq_ready, 4)
            b = begin("cqT")
            for k in range(2):
                for a in range(TT):
                    ins = t_.transpose(b[:, k * T + a * P:k * T + (a + 1) * P], u_tok[:, a, k * P:(k + 1) * P], ident[:, :])
            end("cqT", ins)
            b = begin("ckvT")
            for a in range(TT):
                ins = t_.transpose(b[:, a * P:(a + 1) * P], u_tok[:, a, Q_LORA:Q_LORA + KV_LORA], ident[:, :])
            end("ckvT", ins)
            b = begin("krT")
            pe.wait_ge(krow_ready, 1)
            for a in range(TT):
                ins = t_.transpose(b[0:QK, a * P:(a + 1) * P], krow[:, a, :], ident[:, :])
            end("krT", ins)
            wait_drained(pe, "cqT")
            pe.wait_ge(loaded["uq"], 16)
            for t in range(TT):
                for h in range(2):
                    b = begin(f"q{t}{h}")
                    for k in range(2):
                        ins = t_.matmul(b[:, 0:4 * QK], cqT[:, k, t * P:(t + 1) * P],
                                        uq_sb[:, k, h * 4 * QK:(h + 1) * 4 * QK], start=k == 0, stop=k == 1)
                    end(f"q{t}{h}", ins)
            wait_drained(pe, "ckvT")
            pe.wait_ge(loaded["ukv"], 16)
            for i in range(4):
                b = begin(f"kn{i}")
                for h in range(2):
                    ins = t_.matmul(b[0:NOPE, h * T:(h + 1) * T], ukv_sb[:, 2 * i + h, 0:NOPE], ckvT, start=True, stop=True)
                end(f"kn{i}", ins)
            for t in range(TT):
                b = begin(f"v{t}")
                end(f"v{t}", t_.matmul(b[:, :], ckvT[:, t * P:(t + 1) * P], ukv_sb[:, :, NOPE:], start=True, stop=True))
            pe.wait_ge(q_ready, TT)
            for i in range(4):
                b = begin(f"qT{i}")
                for h in range(2):
                    for a in range(TT):
                        ins = t_.transpose(b[0:QK, h * T + a * P:h * T + (a + 1) * P], q_tok[:, a, 2 * i + h, :], ident[:, :])
                end(f"qT{i}", ins)
            wait_drained(pe, "qT3")
            wait_drained(pe, "kn3")
            for i in range(2):
                b = begin(f"s0{i}")
                for h in range(4):
                    ins = t_.matmul(b[:, h * P:(h + 1) * P], qTs[0:QK, 4 * i + h, 0:P], KTs[0:QK, 4 * i + h, 0:P],
                                    start=True, stop=True)
                end(f"s0{i}", ins)
            for i in range(4):
                b = begin(f"s1{i}")
                for h in range(2):
                    ins = t_.matmul(b[:, h * T:(h + 1) * T], qTs[0:QK, 2 * i + h, P:T], KTs[0:QK, 2 * i + h, :],
                                    start=True, stop=True)
                end(f"s1{i}", ins)
            key_job(2)
            key_job(3)
            pe.wait_ge(e_ready, 1)
            for i in range(2):
                b = begin(f"pT0{i}")
                for h in range(4):
                    ins = t_.transpose(b[:, h * P:(h + 1) * P], S0[:, 4 * i + h, :], ident[:, :])
                end(f"pT0{i}", ins)
            pe.wait_ge(e_ready, 2)
            for i in range(4):
                b = begin(f"pT1{i}")
                for h in range(2):
                    for a in range(2):
                        ins = t_.transpose(b[:, (2 * h + a) * P:(2 * h + a + 1) * P],
                                           S1[:, 2 * i + h, a * P:(a + 1) * P], ident[:, :])
                end(f"pT1{i}", ins)
            wait_drained(pe, "pT13")
            for t in range(TT):
                b = begin(f"o{t}")
                for h in range(HEADS):
                    for a in range(t + 1):
                        lhs = PT0[:, h, :] if t == 0 else PT1[:, h, a, :]
                        ins = t_.matmul(b[:, h * VDIM:(h + 1) * VDIM], lhs, Vs[:, a, h * VDIM:(h + 1) * VDIM],
                                        start=a == 0, stop=a == t)
                end(f"o{t}", ins)
            value_job(0)
            wait_drained(pe, "o1")
            for t in range(TT):
                b = begin(f"oT{t}")
                for k in range(4):
                    ins = t_.transpose(b[:, k * P:(k + 1) * P], o_tok[:, t, k * P:(k + 1) * P], ident[:, :])
                end(f"oT{t}", ins)
            pe.wait_ge(loaded["wout"], 16)
            wait_drained(pe, "oT1")
            wb = {(t, n): begin(f"w{t}{n}") for t in range(TT) for n in range(2)}

            def attention_half(t, n):
                for k in range(4):
                    t_.matmul(wb[t, n][:, :], yT[:, k, t * P:(t + 1) * P], wout_sb[:, k, n * BANK:(n + 1) * BANK],
                              start=k == 0, stop=False)

            attention_half(0, 0)
            attention_half(0, 1)
            attention_half(1, 0)
            b = begin("mean")
            pe.wait_ge(const_ready, N_CONST)
            pe.wait_ge(conv_step, TAPS * CONV_V)
            pe.wait_ge(conv_pool_step, TAPS * (CT - CONV_V))
            for c in range(CT):
                ins = t_.matmul(b[:, 0:T], mean_w[:, :], acc[:, c, :], start=c == 0, stop=c == CT - 1)
            end("mean", ins)
            attention_half(1, 1)
            b = begin("var")
            pe.wait_ge(zsq_ready, 1)
            for c in range(CT):
                ins = t_.matmul(b[:, 0:T], mean_w[:, :], sq4[:, c, :], start=c == 0, stop=c == CT - 1)
            end("var", ins)
            value_job(1)
            value_job(2)
            pe.wait_ge(yconv_ready, 1)
            for t in range(TT):
                for n in range(2):
                    for k in range(4, KT):
                        ins = t_.matmul(wb[t, n][:, :], yT[:, k, t * P:(t + 1) * P], wout_sb[:, k, n * BANK:(n + 1) * BANK],
                                        start=False, stop=k == KT - 1)
                    end(f"w{t}{n}", ins)

            def residual_transposes(jobs, t):
                for i in range(2):
                    b = begin(f"{jobs}{t}{i}")
                    for k in range(4):
                        at = (4 * i + k) * P
                        ins = t_.transpose(b[:, k * P:(k + 1) * P], xs[:, t, at:at + P], ident[:, :])
                    end(f"{jobs}{t}{i}", ins)

            wait_drained(pe, "w01")
            residual_transposes("h2T", 0)
            wait_drained(pe, "w11")
            residual_transposes("h2T", 1)
            for i in range(4):
                b = begin(f"xq{i}")
                for j in range(2):
                    for k in range(KT):
                        wait_drained(pe, f"h2T1{k // 4}")
                        pe.wait_ge(loaded[f"wxq{k // 4}"], 16)
                        at = (2 * i + j) * P
                        ins = t_.matmul(b[:, j * T:(j + 1) * T], wxq_sb[:, k, at:at + P], h2T[:, k, :],
                                        start=k == 0, stop=k == KT - 1)
                end(f"xq{i}", ins)
            for t in range(TT):
                for g in range(2):
                    b = begin(f"xs{t}{g}")
                    for h in range(2):
                        wait_drained(pe, f"xq{2 * g + h}")
                        for k in range(2):
                            c = 2 * (2 * g + h) + k
                            ins = t_.matmul(b[:, h * M:(h + 1) * M], qT2[:, c, t * P:(t + 1) * P], kTm[:, c, :],
                                            start=k == 0, stop=k == 1)
                    end(f"xs{t}{g}", ins)
            value_job(3)
            for t in range(TT):
                pe.wait_ge(px_ready, t + 1)
                for g in range(2):
                    b = begin(f"xp{t}{g}")
                    for h in range(2):
                        for a in range(2):
                            ins = t_.transpose(b[:, (2 * h + a) * P:(2 * h + a + 1) * P],
                                               px[:, t, 2 * g + h, a * P:(a + 1) * P], ident[:, :])
                    end(f"xp{t}{g}", ins)
            wait_drained(pe, "xp11")
            wait_drained(pe, "xv3")
            for i in range(4):
                b = begin(f"xo{i}")
                for j in range(2):
                    for a in range(2):
                        c = 2 * i + j
                        ins = t_.matmul(b[:, j * T:(j + 1) * T], vm[:, a, c * P:(c + 1) * P], ptx[:, c // 2, a, :],
                                        start=a == 0, stop=a == 1)
                end(f"xo{i}", ins)
            pe.wait_ge(loaded["wxo"], 16)
            for t in range(TT):
                for n in range(2):
                    b = begin(f"wo{t}{n}")
                    for k in range(KT):
                        wait_drained(pe, f"xo{k // 2}")
                        ins = t_.matmul(b[:, :], oT2[:, k, t * P:(t + 1) * P], wxo_sb[:, k, n * BANK:(n + 1) * BANK],
                                        start=k == 0, stop=k == KT - 1)
                    end(f"wo{t}{n}", ins)
            wait_drained(pe, "wo01")
            residual_transposes("tT", 0)
            wait_drained(pe, "wo11")
            residual_transposes("tT", 1)
            pe.wait_ge(loaded["router"], 32)
            for t in range(TT):
                b = begin(f"lg{t}")
                wait_drained(pe, f"tT{t}1")
                for k in range(KT):
                    ins = t_.matmul(b[:, 0:E], tT[:, k, t * P:(t + 1) * P], wr3[:, k, :], start=k == 0, stop=k == KT - 1)
                end(f"lg{t}", ins)
            pick = rt[:, 64:128].rearrange("p (a e) -> p a e", a=TT)
            pe.wait_ge(picks_ready, 2)
            b = begin("count")
            t_.matmul(b[0:E, 0:1], pick[:, 0, :], ones[:, 0:1], start=True, stop=False)
            end("count", t_.matmul(b[0:E, 0:1], pick[:, 1, :], ones[:, 0:1], start=False, stop=True))
            b = begin("rank")
            t_.matmul(b[:, 0:E], before[:, :], pick[:, 0, :], start=True, stop=True)
            t_.matmul(b[:, E:2 * E], ones[:, :], pick[:, 0, :], start=True, stop=False)
            end("rank", t_.matmul(b[:, E:2 * E], before[:, :], pick[:, 1, :], start=False, stop=True))
            b = begin("meta")
            wait_drained(pe, "count")
            end("meta", t_.matmul(b[0:1, 0:2 * E], rt[0:E, 308:309], sel32[0:E, :], start=True, stop=True))
            def gather(b):
                pe.wait_ge(p2_ready, b * 2 + 2)
                for a in range(TT):
                    for h in range(2):
                        ins = t_.matmul(banks[4][h * 64:(h + 1) * 64, :], P2v[:, a, h * 64:(h + 1) * 64],
                                        rows[:, a, 4 * h:4 * h + 4, :], start=a == 0, stop=a == 1)
                ins.then_inc(g_full, 1)

            def gather_columns(b):
                pe.wait_ge(g_copied, b + 1)
                for c in range(4):
                    ins = t_.transpose(banks[2][:, c * P:(c + 1) * P], G_sb[:, c * P:(c + 1) * P], ident[:, :])
                ins.then_inc(x_full, 1)

            def combine():
                for a in range(TT):
                    for h in range(2):
                        t_.matmul(banks[COMBINE[2 * a + h]][:, :], PT2[h * 64:(h + 1) * 64, a * P:(a + 1) * P],
                                  y_sb[h * 64:(h + 1) * 64, :], start=True, stop=True).then_inc(c_full, 1)

            pe.wait_ge(rows_ready, TT)
            gather(0)
            b = begin("gT")
            pe.wait_ge(gates_ready, 1)
            t_.transpose(b[:, 0:P], gates2[:, 0, :], ident[:, :]).then_inc(pt_full, 1)
            end("gT", t_.transpose(b[:, P:T], gates2[:, 1, :], ident[:, :]))

            wait_drained(pe, "meta")
            wait_drained(pe, "gT")
            pe.wait_ge(loaded["bdown"], 32)

            gather_columns(0)
            with pe.Fori(0, E // 2) as pair:
                for odd in range(2):
                    e = pair * 2 + odd
                    up0 = 0 if odd else 8
                    extra = pe.value_load(meta_i[0:1, bass.ds(e, 1)], min_val=0, max_val=T // CAP - 1)
                    first = pe.value_load(meta_i[0:1, bass.ds(e + E, 1)], min_val=0, max_val=E + T * TOPK // CAP)
                    with pe.Fori(0, pe.snap(extra + 1)) as r:
                        n = pe.snap(first + r)
                        pe.wait_ge(xg_ready, n + 1)
                        for k in range(KT):
                            pe.wait_ge(slab_in[up0 + k], pair * 16 + 16)
                            w = slab(up0 + k)
                            for c in range(2):
                                for h in range(2):
                                    ins = t_.matmul(banks[c][h * 64:(h + 1) * 64, :], xg[:, k, :],
                                                    w[:, h * FF + c * BANK:h * FF + (c + 1) * BANK],
                                                    start=k == 0, stop=k == KT - 1)
                            ins.then_inc(up_steps, 1)
                        pe.wait_ge(y_ready, n + 1)
                        pe.wait_ge(pt_copied, n + 1)
                        pe.wait_ge(y_added, n * 4 + 1)
                        combine()
                        pe.wait_ge(u_by_a, n + 1)
                        pe.wait_ge(u_by_v, n + 1)
                        for j in range(KT):
                            ins = t_.transpose(banks[2 + j // 4][:, (j % 4) * P:(j % 4 + 1) * P], U_sb[:, j, :], ident[:, :])
                            if j % 4 == 3:
                                ins.then_inc(t_full, 1)
                        pe.wait_ge(cols_ready, n + 1)
                        pe.wait_ge(y_added, n * 4 + 2)
                        for a in range(TT):
                            t_.transpose(banks[6][:, a * P:(a + 1) * P], P2v[:, a, :], ident[:, :])
                        for a in range(TT):
                            ins = t_.matmul(banks[6][:, T:T + 1], P2v[:, a, :], cols[:, 2 + a:3 + a], start=a == 0, stop=a == 1)
                        ins.then_inc(pt_full, 1)
                        pe.wait_ge(y_added, n * 4 + 5)
                        for j in range(KT):
                            if j == 2:
                                gather(n + 1)
                            if j == 6:
                                gather_columns(n + 1)
                            pe.wait_ge(act_ready, n * 2 + (j // 4 + 1))
                            if j % 2 == 0:
                                pe.wait_ge(slab_in[16 + j // 2], e * 16 + 16)
                            w = slab(16 + j // 2)[:, (j % 2) * D:(j % 2 + 1) * D]
                            for h in range(2):
                                ins = t_.matmul(banks[5][h * 64:(h + 1) * 64, :], actT[:, j, :], w[:, h * BANK:(h + 1) * BANK],
                                                start=j == 0, stop=j == KT - 1)
                            if j % 2 == 1:
                                ins.then_inc(down_steps, 1)
            last_b = pe.value_load(meta_i[0:1, 2 * E - 1:2 * E], min_val=0, max_val=E + T * TOPK // CAP)
            last_r = pe.value_load(meta_i[0:1, E - 1:E], min_val=0, max_val=T // CAP - 1)
            blocks = pe.snap(last_b + last_r + 1)
            pe.wait_ge(y_ready, blocks + 1)
            pe.wait_ge(y_added, blocks * 4 + 1)
            combine()


_INS = ['x', 'mem', 'positions', 'g_mix', 'w_in', 'g_q', 'w_uq', 'g_kv', 'w_ukv', 'w_dw', 'b_dw', 'g_conv_ln',
        'b_conv_ln', 'w_out', 'g_xattn', 'g_mem', 'w_xq', 'w_xkv', 'w_xo', 'g_ffn', 'w_router', 'b_router',
        'w_up', 'b_up', 'w_down', 'b_down', 'g_final']


def kernel(**inputs):
    import concourse.bacc as bacc
    from concourse.bass_utils import run_bass_kernel_spmd

    nc = bacc.Bacc("TRN2", target_bir_lowering=False, num_devices=1)
    arrays, args = {}, []
    for name in _INS:
        a = np.ascontiguousarray(inputs[name])
        arrays[f"in_{name}_dram"] = a
        args.append(nc.dram_tensor(f"in_{name}_dram", a.shape, mybir.dt.from_np(a.dtype), kind="ExternalInput").ap())
    args.append(nc.dram_tensor("out_dram", (1, T, D), mybir.dt.float32, kind="ExternalOutput").ap())
    build_program(nc, *args)
    r = run_bass_kernel_spmd(nc, [arrays], core_ids=[0])
    return r.results[0]["out_dram"]
```
